# Optimizing a Trainium2 kernel written in Bass

```python
import jax, jax.numpy as jnp
from jax import lax
import numpy as np

D_MODEL = 1024
BATCH = 1
SEQ = 512
DEPTH = 2

GRID_W = 64
CTX_LEN = 256

N_MIXERS = 2
N_LRU_LAYERS = (DEPTH + 1) // 2
N_ATTN_LAYERS = DEPTH // 2

D_RNN = 1280
LRU_BLOCKS = 16
LRU_BLOCK = D_RNN // LRU_BLOCKS
CONV_W = 4
CONV_PAD = (2, 1)
LRU_C = 8.0

N_Q_HEADS = 8
N_KV_HEADS = 2
HEAD_DIM = 128
Q_PER_KV = N_Q_HEADS // N_KV_HEADS
Q_WIDTH = N_Q_HEADS * HEAD_DIM
KV_WIDTH = N_KV_HEADS * HEAD_DIM
AXIS_DIM = HEAD_DIM // 2
ROPE_THETA = 10000.0
Q_BLOCK = 128

PEER_HEADS = 8
N_KEYS = 128
N_EXPERTS = N_KEYS * N_KEYS
D_KEY = 256
D_KEY_HALF = D_KEY // 2
PEER_TOPK = 16
PEER_CHUNK = 128

DEEPNORM_ALPHA = (2 * DEPTH) ** 0.25
DEEPNORM_BETA = (8 * DEPTH) ** -0.25
LN_EPS = 1e-6
RMS_EPS = 1e-6

kernel_name = "hybrid_rglru_gqa_peer_dit"

F32 = jnp.float32

def _layer_norm(x, g, b):
    xf = x.astype(F32)
    mu = jnp.mean(xf, axis=-1, keepdims=True)
    var = jnp.mean(jnp.square(xf - mu), axis=-1, keepdims=True)
    return ((xf - mu) * lax.rsqrt(var + LN_EPS) * g + b).astype(x.dtype)

def _rms_norm(x, g):
    xf = x.astype(F32)
    return (xf * lax.rsqrt(jnp.mean(xf * xf, axis=-1, keepdims=True) + RMS_EPS) * g).astype(x.dtype)

def _post_norm(res, delta, g, b):
    return _layer_norm(DEEPNORM_ALPHA * res + delta, g, b)

def _modulation(cond, w, b):
    m = jax.nn.silu(cond) @ w + b
    return jnp.split(m[..., None, :], 6, axis=-1)

def _dwconv_centred(x, w, b):
    out = lax.conv_general_dilated(x, w[:, None, :].astype(x.dtype), window_strides=(1,), padding=(CONV_PAD,),
                                   dimension_numbers=('NWC', 'WIO', 'NWC'), feature_group_count=x.shape[-1])
    return out + b

def _rglru_coeffs(xr, gate_w, gate_b, lam):
    bsz, n = xr.shape[:2]
    xb = xr.reshape(bsz, n, LRU_BLOCKS, LRU_BLOCK)
    gates = jnp.einsum('blnd,nde->blne', xb, gate_w) + gate_b
    r = jax.nn.sigmoid(gates[..., :LRU_BLOCK].astype(F32)).reshape(bsz, n, D_RNN)
    i = jax.nn.sigmoid(gates[..., LRU_BLOCK:].astype(F32)).reshape(bsz, n, D_RNN)
    log_a = -LRU_C * r * jax.nn.softplus(-lam.astype(F32))
    a = jnp.exp(log_a)
    b = jnp.sqrt(-jnp.expm1(2.0 * log_a)) * i * xr.astype(F32)
    return a, b

def _linear_scan(a, b, h0):
    b = b.at[:, 0].add(a[:, 0] * h0)

    def combine(lhs, rhs):
        return lhs[0] * rhs[0], rhs[0] * lhs[1] + rhs[1]

    return lax.associative_scan(combine, (a, b), axis=1)[1]

def _rglru_mixer(h_ctx, h_lat, w_in, conv_w, conv_b, gate_w, gate_b, lam, w_out, need_ctx):
    def branches(h):
        gate, xr = jnp.split(h @ w_in, 2, axis=-1)
        return jax.nn.gelu(gate, approximate=False), _dwconv_centred(xr, conv_w, conv_b)

    gate_c, x_c = branches(h_ctx)
    gate_l, x_l = branches(h_lat)
    ys_c, ys_l = [], []
    for d in range(2):
        a_c, b_c = _rglru_coeffs(x_c, gate_w[d], gate_b[d], lam[d])
        a_l, b_l = _rglru_coeffs(x_l, gate_w[d], gate_b[d], lam[d])
        if d == 1:
            a_c, b_c, a_l, b_l = (jnp.flip(t, axis=1) for t in (a_c, b_c, a_l, b_l))
        h_c = _linear_scan(a_c, b_c, jnp.zeros_like(b_c[:, 0]))
        h_l = _linear_scan(a_l, b_l, h_c[:, -1])
        if d == 1:
            h_c, h_l = jnp.flip(h_c, axis=1), jnp.flip(h_l, axis=1)
        ys_c.append(h_c)
        ys_l.append(h_l)
    y_l = ((ys_l[0] + ys_l[1]).astype(h_lat.dtype) * gate_l) @ w_out
    y_c = (((ys_c[0] + ys_c[1]).astype(h_ctx.dtype) * gate_c) @ w_out) if need_ctx else None
    return y_c, y_l

def _axial_rope_tables(rows):
    row, col = jnp.meshgrid(jnp.arange(rows), jnp.arange(GRID_W), indexing='ij')
    pos = jnp.stack([row.reshape(-1), col.reshape(-1)], axis=-1).astype(F32)
    inv_freq = ROPE_THETA ** (-jnp.arange(0, AXIS_DIM, 2, dtype=F32) / AXIS_DIM)
    ang = pos[:, :, None] * inv_freq
    return jnp.cos(ang), jnp.sin(ang)

def _apply_axial_rope(x, cos, sin):
    bsz, n, nh, _ = x.shape
    xf = x.astype(F32).reshape(bsz, n, nh, 2, 2, AXIS_DIM // 2)
    x1, x2 = xf[..., 0, :], xf[..., 1, :]
    c, s = cos[None, :, None], sin[None, :, None]
    out = jnp.stack([x1 * c - x2 * s, x2 * c + x1 * s], axis=-2)
    return out.reshape(x.shape).astype(x.dtype)

def _sdpa(q, k, v):
    s = jnp.einsum('bqhgd,blhd->bhgql', q, k, preferred_element_type=F32) * (HEAD_DIM ** -0.5)
    p = jax.nn.softmax(s, axis=-1).astype(v.dtype)
    return jnp.einsum('bhgql,blhd->bqhgd', p, v)

def _attention_mixer(h_ctx, h_lat, w_qkv, q_gain, k_gain, w_out, cos, sin, need_ctx):
    def project(h):
        bsz, n = h.shape[:2]
        q, k, v = jnp.split(h @ w_qkv, [Q_WIDTH, Q_WIDTH + KV_WIDTH], axis=-1)
        q = _rms_norm(q.reshape(bsz, n, N_Q_HEADS, HEAD_DIM), q_gain)
        k = _rms_norm(k.reshape(bsz, n, N_KV_HEADS, HEAD_DIM), k_gain)
        return q, k, v.reshape(bsz, n, N_KV_HEADS, HEAD_DIM)

    q_c, k_c, v_c = project(h_ctx)
    q_l, k_l, v_l = project(h_lat)
    q_l = _apply_axial_rope(q_l, cos, sin)
    k_l = _apply_axial_rope(k_l, cos, sin)
    k_all = jnp.concatenate([k_l, k_c], axis=1)
    v_all = jnp.concatenate([v_l, v_c], axis=1)
    bsz, n = h_lat.shape[:2]
    n_blk = n // Q_BLOCK
    q_blocks = q_l.reshape(bsz, n_blk, Q_BLOCK, N_KV_HEADS, Q_PER_KV, HEAD_DIM).transpose(1, 0, 2, 3, 4, 5)
    o_l = lax.map(lambda qb: _sdpa(qb, k_all, v_all), q_blocks)
    o_l = o_l.transpose(1, 0, 2, 3, 4, 5).reshape(bsz, n, Q_WIDTH)
    y_l = o_l @ w_out
    if need_ctx:
        n_c = h_ctx.shape[1]
        o_c = _sdpa(q_c.reshape(bsz, n_c, N_KV_HEADS, Q_PER_KV, HEAD_DIM), k_c, v_c).reshape(bsz, n_c, Q_WIDTH)
        y_c = o_c @ w_out
    else:
        y_c = None
    return y_c, y_l

def _peer(h, w_q, sub_keys, u_tab, v_tab):
    def chunk_fn(hc):
        q = (hc @ w_q).reshape(hc.shape[0], PEER_HEADS, 2, D_KEY_HALF)
        s = jnp.einsum('chpd,pnd->chpn', q.astype(F32), sub_keys.astype(F32))
        s1, i1 = lax.top_k(s[:, :, 0], PEER_TOPK)
        s2, i2 = lax.top_k(s[:, :, 1], PEER_TOPK)
        cand_s = (s1[..., :, None] + s2[..., None, :]).reshape(hc.shape[0], PEER_HEADS, PEER_TOPK * PEER_TOPK)
        cand_i = (i1[..., :, None] * N_KEYS + i2[..., None, :]).reshape(hc.shape[0], PEER_HEADS, PEER_TOPK * PEER_TOPK)
        top_s, pos = lax.top_k(cand_s, PEER_TOPK)
        idx = jnp.take_along_axis(cand_i, pos, axis=-1)
        g = jax.nn.softmax(top_s, axis=-1)
        u = jnp.take(u_tab, idx, axis=0)
        act = jax.nn.gelu(jnp.einsum('chkd,cd->chk', u, hc).astype(F32), approximate=False)
        w = (g * act).astype(hc.dtype)
        return jnp.einsum('chk,chkd->cd', w, jnp.take(v_tab, idx, axis=0))

    out = lax.map(chunk_fn, h.reshape(-1, PEER_CHUNK, h.shape[-1]))
    return out.reshape(h.shape)

def setup_inputs(seed: int = 0) -> dict:
    key = jax.random.key(seed)
    ks = jax.random.split(key, 24)

    def nrm(k, shape, scale):
        return scale * jax.random.normal(k, shape, F32)

    u_lam = jax.random.uniform(ks[13], (N_LRU_LAYERS, 2, D_RNN), F32, 0.9, 0.999)
    a0 = u_lam ** (1.0 / LRU_C)
    return {
        'x': nrm(ks[0], (BATCH, SEQ, D_MODEL), 1.0),
        'c': nrm(ks[1], (BATCH, D_MODEL), 1.0),
        'ctx': nrm(ks[2], (BATCH, CTX_LEN, D_MODEL), 1.0),
        'c_ctx': nrm(ks[3], (D_MODEL,), 1.0),
        'mod_w': nrm(ks[4], (DEPTH, D_MODEL, 6 * D_MODEL), D_MODEL ** -0.5),
        'mod_b': nrm(ks[5], (DEPTH, 6 * D_MODEL), 0.02),
        'ln_g': 1.0 + nrm(ks[6], (DEPTH, 2, D_MODEL), 0.02),
        'ln_b': nrm(ks[7], (DEPTH, 2, D_MODEL), 0.02),
        'lru_w_in': nrm(ks[8], (N_LRU_LAYERS, D_MODEL, 2 * D_RNN), D_MODEL ** -0.5),
        'lru_conv_w': nrm(ks[9], (N_LRU_LAYERS, CONV_W, D_RNN), CONV_W ** -0.5),
        'lru_conv_b': nrm(ks[10], (N_LRU_LAYERS, D_RNN), 0.02),
        'lru_gate_w': nrm(ks[11], (N_LRU_LAYERS, 2, LRU_BLOCKS, LRU_BLOCK, 2 * LRU_BLOCK), LRU_BLOCK ** -0.5),
        'lru_gate_b': nrm(ks[12], (N_LRU_LAYERS, 2, LRU_BLOCKS, 2 * LRU_BLOCK), 0.02),
        'lru_lambda': jnp.log(a0) - jnp.log1p(-a0),
        'lru_w_out': nrm(ks[14], (N_LRU_LAYERS, D_RNN, D_MODEL), DEEPNORM_BETA * D_RNN ** -0.5),
        'attn_w_qkv': nrm(ks[15], (N_ATTN_LAYERS, D_MODEL, Q_WIDTH + 2 * KV_WIDTH), D_MODEL ** -0.5),
        'attn_q_gain': 1.0 + nrm(ks[16], (N_ATTN_LAYERS, HEAD_DIM), 0.02),
        'attn_k_gain': 1.0 + nrm(ks[17], (N_ATTN_LAYERS, HEAD_DIM), 0.02),
        'attn_w_out': nrm(ks[18], (N_ATTN_LAYERS, Q_WIDTH, D_MODEL), DEEPNORM_BETA * Q_WIDTH ** -0.5),
        'peer_w_q': nrm(ks[19], (DEPTH, D_MODEL, PEER_HEADS * D_KEY), D_MODEL ** -0.5),
        'peer_sub_keys': nrm(ks[20], (DEPTH, 2, N_KEYS, D_KEY_HALF), D_KEY_HALF ** -0.5),
        'peer_u': nrm(ks[21], (DEPTH, N_EXPERTS, D_MODEL), D_MODEL ** -0.5),
        'peer_v': nrm(ks[22], (DEPTH, N_EXPERTS, D_MODEL), DEEPNORM_BETA),
    }

def reference(x, c, ctx, c_ctx, mod_w, mod_b, ln_g, ln_b, lru_w_in, lru_conv_w, lru_conv_b, lru_gate_w,
              lru_gate_b, lru_lambda, lru_w_out, attn_w_qkv, attn_q_gain, attn_k_gain, attn_w_out,
              peer_w_q, peer_sub_keys, peer_u, peer_v):
    d = x.shape[-1]
    rows = x.shape[1] // GRID_W
    cos, sin = _axial_rope_tables(rows)
    for i in range(DEPTH):
        need_ctx = i < DEPTH - 1
        sh1, sc1, g1, sh2, sc2, g2 = _modulation(c, mod_w[i], mod_b[i])
        csh1, csc1, cg1, csh2, csc2, cg2 = _modulation(c_ctx, mod_w[i], mod_b[i])
        h_lat = x * (1.0 + sc1) + sh1
        h_ctx = ctx * (1.0 + csc1) + csh1
        j = i // N_MIXERS
        if i % N_MIXERS == 0:
            y_ctx, y_lat = _rglru_mixer(h_ctx, h_lat, lru_w_in[j], lru_conv_w[j], lru_conv_b[j], lru_gate_w[j],
                                        lru_gate_b[j], lru_lambda[j], lru_w_out[j], need_ctx)
        else:
            y_ctx, y_lat = _attention_mixer(h_ctx, h_lat, attn_w_qkv[j], attn_q_gain[j], attn_k_gain[j],
                                            attn_w_out[j], cos, sin, need_ctx)
        x = _post_norm(x, g1 * y_lat, ln_g[i, 0], ln_b[i, 0])
        f_lat = _peer((x * (1.0 + sc2) + sh2).reshape(-1, d), peer_w_q[i], peer_sub_keys[i], peer_u[i], peer_v[i])
        x = _post_norm(x, g2 * f_lat.reshape(x.shape), ln_g[i, 1], ln_b[i, 1])
        if need_ctx:
            ctx = _post_norm(ctx, cg1 * y_ctx, ln_g[i, 0], ln_b[i, 0])
            f_ctx = _peer((ctx * (1.0 + csc2) + csh2).reshape(-1, d), peer_w_q[i], peer_sub_keys[i], peer_u[i], peer_v[i])
            ctx = _post_norm(ctx, cg2 * f_ctx.reshape(ctx.shape), ln_g[i, 1], ln_b[i, 1])
    return x


_drawn_inputs = setup_inputs


def setup_inputs(seed=0):
    import zlib

    import numpy as np

    out = dict(_drawn_inputs(seed))
    spreads = {}
    factors = {'lru_gate_b': 3.568, 'attn_q_gain': 8.0, 'attn_k_gain': 8.0}
    for name, (base, spread) in spreads.items():
        noise = np.random.default_rng([zlib.crc32(name.encode()), seed]).standard_normal(out[name].shape)
        drawn = base * np.exp(spread * noise) if base else spread * noise
        out[name] = __import__('jax').numpy.asarray(drawn.astype(out[name].dtype))
    for name, factor in factors.items():
        out[name] = (out[name] * factor).astype(out[name].dtype)
    return out
```

```python
from contextlib import ExitStack

import concourse.bass as bass
import numpy as np
from concourse import mybir

F32 = mybir.dt.float32
U32 = mybir.dt.uint32
ALU = mybir.AluOpType
ACT = mybir.ActivationFunctionType
AX_X = mybir.AxisListType.X
ds = bass.ds

P = 128
D = 1024
KC = D // P
CTX = 256
SEQ = 512
TOK = CTX + SEQ
TILES = TOK // P
CTX_TILES = CTX // P
DEPTH = 2
MOD = 6 * D
SH1, SC1, G1, SH2, SC2, G2 = range(6)
LAT, CON = 0, 1

D_RNN = 1280
LB = 80
NB = D_RNN // LB
TAPS = 4
PAD_L, PAD_R = 2, 1
COLS = TAPS + 1 + 4 + 2
LRU_C = 8.0

HEADS = 8
KV = 2
HD = 128

PH = 8
NK = 128
TOPK = 16
EXPERTS = NK * NK
ROW = 2 * D
RING = 16
BATCH = 4

ALPHA = float((2 * DEPTH) ** 0.25)
EPS = 1e-6
LOWEST = -3.0e38

HALF = 512


class Counter:

    def __init__(self, sem):
        self.sem, self.base, self.n = sem, 0, 0

    def loop(self, i, per):
        self.start = self.base + self.n
        self.per = per
        self.base, self.n = self.start + i * per, 0

    def end(self, rounds):
        assert self.n == self.per, (self.n, self.per)
        self.base, self.n = self.start + rounds * self.per, 0

    def mark(self, ins):
        self.n += 1
        ins.then_inc(self.sem, 1)

    def wait(self, eng, back=0):
        eng.wait_ge(self.sem, self.base + (self.n - back))

    def link(self, eng, ins):
        self.n += 1
        ins.then_inc(self.sem, 1)
        eng.wait_ge(self.sem, self.base + self.n)


class Stage:

    def __init__(self, nc, name):
        self.nc, self.name, self.stack, self.sems = nc, name, ExitStack(), []

    def __enter__(self):
        self.stack.__enter__()
        return self

    def __exit__(self, *e):
        if e[0] is None:
            self.nc.clear_and_free_semaphores(self.sems)
            self.nc.all_engine_barrier()
        return self.stack.__exit__(*e)

    def sb(self, name, shape, dt=F32):
        return self.stack.enter_context(self.nc.sbuf_tensor(f"{self.name}_{name}", shape, dt))

    def ps(self, name, shape):
        return self.stack.enter_context(self.nc.psum_tensor(f"{self.name}_{name}", shape, F32))

    def sem(self, name):
        self.sems.append(self.nc.alloc_semaphore(f"{self.name}_{name}"))
        return self.sems[-1]

    def pool_dma_sem(self, name):
        return self.nc.alloc_semaphore(f"{self.name}_{name}")


def mod_row(mod, layer, cond, kind):
    at = layer * MOD + kind * D
    return mod[cond:cond + 1, at:at + D].broadcast_to([P, D])


def row_of(vector):
    return vector.rearrange("(a d) -> a d", a=1).broadcast_to([P, D])


def modulation(nc, a, mod):
    CH = MOD // HALF
    NBUF = 4
    w = a["mod_w"].rearrange("l (k p) n -> l p k n", p=P)
    with Stage(nc, "mod") as s:
        cond = s.sb("cond", [P, KC, 2])
        act = s.sb("act", [P, KC, 2])
        wbuf = [s.sb(f"w{u}", [P, KC, HALF]) for u in range(NBUF)]
        bias = s.sb("bias", [2, DEPTH * MOD])
        row = s.sb("row", [2, DEPTH * MOD])
        psum = s.ps("ps", [P, NBUF, HALF])
        cond_in, bias_in, silu_done, plus1 = (s.sem(n) for n in ("cond_in", "bias_in", "silu_done", "plus1"))
        w_in = [s.sem(f"w_in{u}") for u in range(NBUF)]
        mm_done, row_done = s.sem("mm_done"), s.sem("row_done")
        row_out = s.sem("row_out")
        with nc.Block() as block:

            @block.sync
            def _(sp):
                sp.dma_start(cond[:], a["cond"]).then_inc(cond_in, 16)
                sp.dma_start(bias[:], a["mod_b"].rearrange("l n -> (l n)").rearrange("(a n) -> a n", a=1)
                             .broadcast_to([2, DEPTH * MOD])).then_inc(bias_in, 16)
                for layer in range(DEPTH):
                    with sp.Fori(0, CH // NBUF) as i:
                        for u in range(NBUF):
                            sp.wait_ge(mm_done, i * NBUF + (layer * CH + u + 1))
                            sp.dma_start(wbuf[u][:], w[layer, :, :, ds((i * NBUF + u) * HALF, HALF)]).then_inc(w_in[u], 16)
                sp.wait_ge(row_done, NBUF + DEPTH * CH)
                sp.dma_start(mod, row[:]).then_inc(row_out, 16)
                sp.wait_ge(row_out, 16)

            @block.scalar
            def _(act_e):
                act_e.wait_ge(cond_in, 16)
                nc.scalar.activation(act[:], cond[:], ACT.Silu).then_inc(silu_done, 1)

            @block.tensor
            def _(pe):
                pe.sem_inc(mm_done, NBUF)
                pe.wait_ge(silu_done, 1)
                for layer in range(DEPTH):
                    with pe.Fori(0, CH // NBUF) as i:
                        for u in range(NBUF):
                            pe.wait_ge(w_in[u], (i + (layer * (CH // NBUF) + 1)) * 16)
                            pe.wait_ge(row_done, i * NBUF + (layer * CH + u + 1))
                            for k in range(KC):
                                last = nc.tensor.matmul(psum[0:2, u, :], act[:, k, :], wbuf[u][:, k, :],
                                                        start=k == 0, stop=k == KC - 1)
                            last.then_inc(mm_done, 1)

            @block.vector
            def _(dve):
                dve.sem_inc(row_done, NBUF)
                dve.wait_ge(bias_in, 16)
                steps = Counter(plus1)
                for layer in range(DEPTH):
                    for kind in (SC1, SC2):
                        v = bias[:, layer * MOD + kind * D:layer * MOD + (kind + 1) * D]
                        steps.link(dve, nc.vector.tensor_scalar(v, v, 1.0, None, ALU.add))
                for layer in range(DEPTH):
                    with dve.Fori(0, CH // NBUF) as i:
                        for u in range(NBUF):
                            dve.wait_ge(mm_done, i * NBUF + (NBUF + layer * CH + u + 1))
                            at = i * (NBUF * HALF) + (layer * MOD + u * HALF)
                            nc.vector.tensor_tensor(row[:, ds(at, HALF)], psum[0:2, u, :], bias[:, ds(at, HALF)],
                                                    ALU.add).then_inc(row_done, 1)


def modulated_transpose(nc, s, x, ident, ps, layer, a, mod):
    hT = s.sb("hT", [P, KC, TOK])
    sc = s.sb("sc", [P, 2, D])
    sh = s.sb("sh", [P, 2, D])
    h = [s.sb(f"h{u}", [P, D]) for u in range(2)]
    x_in, mod_in, h_step, h_ready, hT_ps, hT_done = (
        s.sem(n) for n in ("x_in", "mod_in", "h_step", "h_ready", "hT_ps", "hT_done"))
    load_x = layer == 0

    def sync(sp):
        for cond in (LAT, CON):
            sp.dma_start(sc[:, cond, :], mod_row(mod, layer, cond, SC1)).then_inc(mod_in, 16)
            sp.dma_start(sh[:, cond, :], mod_row(mod, layer, cond, SH1)).then_inc(mod_in, 16)
        if load_x:
            sp.dma_start(x[:, 0:CTX_TILES, :], a["ctx"].rearrange("(t p) d -> p t d", p=P)).then_inc(x_in, 16)
            sp.dma_start(x[:, CTX_TILES:, :], a["x"].rearrange("(t p) d -> p t d", p=P)).then_inc(x_in, 16)

    def vector(dve):
        dve.wait_ge(mod_in, 64)
        if load_x:
            dve.wait_ge(x_in, 32)
        steps = Counter(h_step)
        for first, pairs, cond in ((0, 1, CON), (1, 2, LAT)):
            with dve.Fori(0, pairs) as i:
                steps.loop(i, 2)
                for u in range(2):
                    if first:
                        dve.wait_ge(hT_ps, i * 2 + (2 * first + u - 1))
                    xt = x[:, ds(i * 2 + (2 * first + u), 1), :].rearrange("p a d -> p (a d)")
                    steps.link(dve, nc.vector.tensor_tensor(h[u][:], xt, sc[:, cond, :], ALU.mult))
                    nc.vector.tensor_tensor(h[u][:], h[u][:], sh[:, cond, :], ALU.add).then_inc(h_ready, 1)
                steps.end(pairs)

    def tensor(pe):
        with pe.Fori(0, TILES // 2) as i:
            for u in range(2):
                pe.wait_ge(h_ready, i * 2 + (u + 1))
                pe.wait_ge(hT_done, i * 2 + (u + 1))
                for k in range(KC):
                    last = nc.tensor.transpose(ps[:, 2 * u + k // 4, (k % 4) * P:(k % 4 + 1) * P],
                                               h[u][:, k * P:(k + 1) * P], ident)
                last.then_inc(hT_ps, 1)

    def scalar(act):
        act.sem_inc(hT_done, 2)
        with act.Fori(0, TILES // 2) as i:
            for u in range(2):
                act.wait_ge(hT_ps, i * 2 + (u + 1))
                nc.scalar.copy(hT[:, :, ds(i * (2 * P) + u * P, P)],
                               ps[:, 2 * u:2 * u + 2, :].rearrange("p b (k c) -> p (b k) c", c=P)).then_inc(hT_done, 1)

    return hT, (hT_done, TILES + 2), sync, vector, tensor, scalar


def lru_mixer(nc, a, mod, mixed, x, ident):
    w_in = a["w_in"]
    with Stage(nc, "lru") as s:
        ps = s.ps("ps", [P, 8, HALF])
        hT, (hT_done, hT_all), front_sync, front_vector, front_tensor, front_scalar = modulated_transpose(
            nc, s, x, ident, ps, 0, a, mod)
        wx = [s.sb(f"wx{u}", [P, KC, 2 * LB]) for u in range(2)]
        wg = [s.sb(f"wg{u}", [LB, 2, 2 * LB]) for u in range(2)]
        cols = s.sb("cols", [LB, NB, COLS])
        gbias = s.sb("gbias", [LB, NB, 4])
        decay = s.sb("decay", [LB, NB, 2, 3])
        lam = [s.sb(f"lam{n}", [LB, NB, 2]) for n in range(6)]
        LEN = PAD_L + CTX + PAD_R + PAD_L + SEQ + PAD_R
        LAT0 = CTX + PAD_R + PAD_L
        OUTS = LEN - (TAPS - 1)
        xpad = s.sb("xpad", [LB, LEN])
        conv = s.sb("conv", [LB, OUTS])
        xc = [s.sb(f"xc{u}", [LB, TOK]) for u in range(2)]
        gate = [s.sb(f"gate{u}", [LB, TOK]) for u in range(2)]
        tr, ti, av, a2, th, hs = ([s.sb(f"{n}{d}", [LB, TOK]) for d in range(2)] for n in ("tr", "ti", "av", "a2", "th", "hs"))
        y = [s.sb(f"y{u}", [LB, TOK]) for u in range(2)]
        px, pg, pr, pi = (ps[0:LB, 2 * n:2 * n + 2, :].rearrange("p b n -> p (b n)") for n in range(4))
        cols_in, e_done, prep_step, prep_done = (s.sem(n) for n in ("cols_in", "e_done", "prep_step", "prep_done"))
        w_ld = [s.sem(f"w_ld{u}") for u in range(2)]
        x_ps, g_ps = s.sem("x_ps"), s.sem("g_ps")
        x_copied, gate_done, conv_done, gates_ps, tanh_done, y_done, y_free = (
            s.sem(n) for n in ("x_copied", "gate_done", "conv_done", "gates_ps", "tanh_done", "y_done", "y_free"))
        step, dec_done, v_done, root_done = (s.sem(n) for n in ("step", "dec_done", "v_done", "root_done"))
        y_out = s.pool_dma_sem("y_out")
        halves = ((0, HALF), (HALF, TOK - HALF))

        def col(t, b, *at):
            v = t[:, ds(b, 1), at[0]:at[0] + 1] if len(at) == 1 else t[:, ds(b, 1), at[0], at[1]:at[1] + 1]
            return v.rearrange("p a c -> p (a c)")

        with nc.Block() as block:

            @block.sync
            def _(sp):
                front_sync(sp)
                sp.dma_start(cols[:], a["lru_cols"]).then_inc(cols_in, 16)
                with sp.Fori(0, NB // 2) as i:
                    for u in range(2):
                        sp.wait_ge(gates_ps, i * 4 + (2 * u + 2))
                        sp.dma_start(wx[u][:], w_in[ds(i * 2 + u, 1)].rearrange("b p k n -> (b p) k n")).then_inc(w_ld[u], 16)
                        sp.dma_start(wg[u][:], a["gate_w"][ds(i * 2 + u, 1)].rearrange("b p d n -> (b p) d n")).then_inc(w_ld[u], 16)

            @block.gpsimd
            def _(pool):
                pool.sem_inc(y_free, 2)
                with pool.Fori(0, NB // 2) as i:
                    for u in range(2):
                        pool.wait_ge(y_done, i * 2 + (u + 2))
                        pool.dma_start(mixed[ds(i * (2 * LB) + u * LB, LB), :], y[u][:]).then_inc(y_out, 16)
                        pool.wait_ge(y_out, i * 32 + (16 * u + 16))
                        pool.sem_inc(y_free, 1)

            @block.tensor
            def _(pe):
                pe.sem_inc(gates_ps, 4)
                front_tensor(pe)
                pe.wait_ge(hT_done, hT_all)
                with pe.Fori(0, NB // 2) as i:
                    for u in range(2):
                        b = i * 2 + u
                        pe.wait_ge(w_ld[u], i * 32 + 32)
                        for part, dst, free, done in ((1, px, x_copied, x_ps), (0, pg, gate_done, g_ps)):
                            pe.wait_ge(free, b + 1)
                            for at, n in halves:
                                for k in range(KC):
                                    last = nc.tensor.matmul(dst[:, at:at + n], wx[u][:, k, part * LB:(part + 1) * LB],
                                                            hT[:, k, at:at + n], start=k == 0, stop=k == KC - 1)
                            last.then_inc(done, 1)
                        pe.wait_ge(conv_done, b + 2)
                        for d in range(2):
                            pe.wait_ge(tanh_done, b * 2 + (d + 1))
                            for part, dst in ((0, pr), (1, pi)):
                                for at, n in halves:
                                    last = nc.tensor.matmul(dst[:, at:at + n], wg[u][:, d, part * LB:(part + 1) * LB],
                                                            xc[u][:, at:at + n], start=True, stop=True)
                            last.then_inc(gates_ps, 1)

            @block.scalar
            def _(act):
                act.sem_inc(x_copied, 1)
                act.sem_inc(gate_done, 1)
                act.sem_inc(tanh_done, 1)
                front_scalar(act)
                act.wait_ge(cols_in, 16)
                nc.scalar.activation(lam[0][:], cols[:, :, 9:11], ACT.Abs).then_inc(e_done, 1)
                act.wait_ge(e_done, 1)
                nc.scalar.activation(lam[1][:], lam[0][:], ACT.Exp, scale=-1.0).then_inc(e_done, 1)
                act.wait_ge(prep_done, 1)
                with act.Fori(0, NB // 2) as i:
                    for u in range(2):
                        b = i * 2 + u
                        act.wait_ge(x_ps, b + 1)
                        act.wait_ge(conv_done, b + 1)
                        nc.scalar.copy(xpad[:, PAD_L:PAD_L + CTX], px[:, 0:CTX])
                        nc.scalar.copy(xpad[:, PAD_L + LAT0:PAD_L + LAT0 + SEQ], px[:, CTX:TOK]).then_inc(x_copied, 1)
                        act.wait_ge(g_ps, b + 1)
                        nc.scalar.activation(gate[u][:], pg[:, 0:TOK], ACT.Gelu).then_inc(gate_done, 1)
                        act.wait_ge(y_done, b + 1)
                        for d in range(2):
                            act.wait_ge(gates_ps, b * 2 + (4 + d + 1))
                            nc.scalar.activation(tr[d][:], pr[:, 0:TOK], ACT.Tanh, scale=0.5, bias=col(gbias, b, 2 * d))
                            nc.scalar.activation(ti[d][:], pi[:, 0:TOK], ACT.Tanh, scale=0.5,
                                                 bias=col(gbias, b, 2 * d + 1)).then_inc(tanh_done, 1)
                            act.wait_ge(tanh_done, b * 2 + (d + 2))
                            n, minus, twice = (col(decay, b, d, j) for j in range(3))
                            nc.scalar.activation(av[d][:], tr[d][:], ACT.Exp, scale=n, bias=n)
                            nc.scalar.activation(a2[d][:], tr[d][:], ACT.Exp, scale=twice, bias=twice)
                            nc.scalar.activation(th[d][:], tr[d][:], ACT.Tanh, scale=minus, bias=minus).then_inc(dec_done, 1)
                        for d in range(2):
                            act.wait_ge(v_done, b * 2 + (d + 1))
                            nc.scalar.activation(th[d][:], th[d][:], ACT.Sqrt, scale=0.25).then_inc(root_done, 1)

            @block.vector
            def _(dve):
                dve.sem_inc(y_done, 1)
                nc.vector.memset(xpad[:], 0.0).then_inc(conv_done, 1)
                front_vector(dve)
                dve.wait_ge(cols_in, 16)
                dve.wait_ge(e_done, 2)
                steps = Counter(prep_step)
                e, t, z, p, acc = lam[1], lam[2], lam[3], lam[4], lam[5]
                steps.link(dve, nc.vector.tensor_scalar(t[:], e[:], 2.0, None, ALU.add))
                steps.link(dve, nc.vector.reciprocal(t[:], t[:]))
                steps.link(dve, nc.vector.tensor_tensor(z[:], e[:], t[:], ALU.mult))
                steps.link(dve, nc.vector.tensor_tensor(p[:], z[:], z[:], ALU.mult))
                steps.link(dve, nc.vector.tensor_scalar(acc[:], p[:], 1.0 / 15, None, ALU.mult))
                for n in (13, 11, 9, 7, 5, 3):
                    steps.link(dve, nc.vector.scalar_tensor_tensor(acc[:], acc[:], 1.0 / n, p[:], ALU.add, ALU.mult))
                steps.link(dve, nc.vector.scalar_tensor_tensor(acc[:], acc[:], 1.0, z[:], ALU.add, ALU.mult))
                steps.link(dve, nc.vector.tensor_scalar(t[:], cols[:, :, 9:11], -1.0, 0.0, ALU.mult, ALU.max))
                steps.link(dve, nc.vector.scalar_tensor_tensor(acc[:], acc[:], 2.0, t[:], ALU.mult, ALU.add))
                for j, f in enumerate((-LRU_C / 2, LRU_C / 2, -LRU_C)):
                    nc.vector.tensor_scalar(decay[:, :, :, j], acc[:], f, None, ALU.mult)
                nc.vector.tensor_scalar(gbias[:], cols[:, :, 5:9], 0.5, None, ALU.mult).then_inc(prep_done, 1)
                dve.wait_ge(prep_done, 1)
                main = Counter(step)
                with dve.Fori(0, NB // 2) as i:
                    main.loop(i, 2 * (3 + 2 + 2 + 3 + 1))
                    for u in range(2):
                        b = i * 2 + u
                        dve.wait_ge(x_copied, b + 2)
                        main.link(dve, nc.vector.tensor_scalar(conv[:], xpad[:, 0:OUTS], col(cols, b, 0), col(cols, b, TAPS),
                                                               ALU.mult, ALU.add))
                        for k in (1, 2):
                            main.link(dve, nc.vector.scalar_tensor_tensor(conv[:], xpad[:, k:k + OUTS], col(cols, b, k),
                                                                          conv[:], ALU.mult, ALU.add))
                        dve.wait_ge(gates_ps, b * 2 + 2)
                        k = TAPS - 1
                        for to, at, n in ((0, 0, CTX), (CTX, LAT0, SEQ)):
                            last = nc.vector.scalar_tensor_tensor(xc[u][:, to:to + n], xpad[:, at + k:at + k + n],
                                                                  col(cols, b, k), conv[:, at:at + n], ALU.mult, ALU.add)
                        last.then_inc(conv_done, 1)
                        dve.wait_ge(conv_done, b + 2)
                        for d in range(2):
                            dve.wait_ge(dec_done, b * 2 + (d + 1))
                            nc.vector.scalar_tensor_tensor(th[d][:], a2[d][:], 1.0, th[d][:], ALU.add,
                                                           ALU.mult).then_inc(v_done, 1)
                        for d in range(2):
                            main.link(dve, nc.vector.scalar_tensor_tensor(ti[d][:], ti[d][:], 1.0, xc[u][:], ALU.add, ALU.mult))
                        for d in range(2):
                            dve.wait_ge(root_done, b * 2 + (d + 1))
                            main.link(dve, nc.vector.tensor_tensor(ti[d][:], ti[d][:], th[d][:], ALU.mult))
                        main.link(dve, nc.vector.tensor_tensor_scan(hs[0][:], av[0][:], ti[0][:], 0.0, ALU.mult, ALU.add))
                        main.link(dve, nc.vector.tensor_tensor_scan(hs[1][:, CTX - 1::-1], av[1][:, CTX - 1::-1],
                                                                    ti[1][:, CTX - 1::-1], 0.0, ALU.mult, ALU.add))
                        main.link(dve, nc.vector.tensor_tensor_scan(hs[1][:, TOK - 1:CTX - 1:-1], av[1][:, TOK - 1:CTX - 1:-1],
                                                                    ti[1][:, TOK - 1:CTX - 1:-1], hs[1][:, 0:1], ALU.mult, ALU.add))
                        main.link(dve, nc.vector.tensor_tensor(hs[0][:], hs[0][:], hs[1][:], ALU.add))
                        dve.wait_ge(gate_done, b + 2)
                        dve.wait_ge(y_free, b + 1)
                        nc.vector.tensor_tensor(y[u][:], hs[0][:], gate[u][:], ALU.mult).then_inc(y_done, 1)
                main.end(NB // 2)


def attn_mixer(nc, a, mod, mixed, x, ident):
    PER_KV = HEADS // KV
    QT = SEQ // P
    with Stage(nc, "attn") as s:
        ps = s.ps("ps", [P, 8, HALF])
        hT, (hT_done, hT_all), front_sync, front_vector, front_tensor, front_scalar = modulated_transpose(
            nc, s, x, ident, ps, 1, a, mod)
        wk, wv = s.sb("wk", [P, KC, KV * HD]), s.sb("wv", [P, KC, KV * HD])
        wq = [s.sb(f"wq{u}", [P, KC, HD]) for u in range(2)]
        rope, rot, ones, gains, eps = (s.sb("rope", [P, 2, TOK]), s.sb("rot", [P, P]), s.sb("ones", [P, P]),
                                       s.sb("gains", [P, 2]), s.sb("eps", [P, 1]))
        kT = [s.sb(f"kT{n}", [P, TOK]) for n in range(KV)]
        v = s.sb("v", [P, TILES, KV * HD])
        qT = [s.sb(f"qT{u}", [P, SEQ]) for u in range(2)]
        scaled, square, root, turned = (s.sb(n, [P, HALF]) for n in ("scaled", "square", "root", "turned"))
        p = [s.sb(f"p{u}", [P, TOK]) for u in range(2)]
        pT = s.sb("pT", [P, TILES, SEQ])
        neg_max, total, inv = (s.sb(n, [P, 2]) for n in ("neg_max", "total", "inv"))
        biggest = s.sb("biggest", [P, 2])
        o = [s.sb(f"o{u}", [P, SEQ]) for u in range(2)]
        const_in, ones_done, k_in, v_in = (s.sem(n) for n in ("const_in", "ones_done", "k_in", "v_in"))
        o_out = s.pool_dma_sem("o_out")
        wq_in = [s.sem(f"wq_in{u}") for u in range(2)]
        v_ps, v_copied, proj_ps, scaled_done, sums_ps, root_done, rows_done = (
            s.sem(n) for n in ("v_ps", "v_copied", "proj_ps", "scaled_done", "sums_ps", "root_done", "rows_done"))
        step, s_ps, max_done, norm_done = (s.sem(n) for n in ("step", "s_ps", "max_done", "norm_done"))
        p_done, pT_ps, pT_copied, o_ps, o_copied, o_stored = (
            s.sem(n) for n in ("p_done", "pT_ps", "pT_copied", "o_ps", "o_copied", "o_stored"))
        proj, sums, partner = ps[:, 6, :], ps[:, 7, :], ps[:, 5, :]
        key_parts = ((0, HALF), (HALF, TOK - HALF))
        KEY_ROWS = KV * len(key_parts)
        HEAD_STEPS = 4 + 2 * QT
        SCALE = HD ** -0.5

        def rows_tensor(pe, w, n, tokens, done):
            for k in range(KC):
                last = nc.tensor.matmul(proj[:, 0:n], w(k), hT[:, k, tokens:tokens + n], start=k == 0, stop=k == KC - 1)
            last.then_inc(proj_ps, 1)
            pe.wait_ge(scaled_done, done)
            nc.tensor.matmul(sums[:, 0:n], ones[:], square[:, 0:n], start=True, stop=True)
            nc.tensor.matmul(partner[:, 0:n], rot[:], scaled[:, 0:n], start=True, stop=True).then_inc(sums_ps, 1)

        def rows_scalar(act, which, n, done):
            act.wait_ge(proj_ps, done)
            nc.scalar.mul(scaled[:, 0:n], proj[:, 0:n], gains[:, which:which + 1])
            nc.scalar.activation(square[:, 0:n], proj[:, 0:n], ACT.Square).then_inc(scaled_done, 1)
            act.wait_ge(sums_ps, done)
            nc.scalar.activation(root[:, 0:n], sums[:, 0:n], ACT.Sqrt, bias=eps[:], scale=1.0 / HD).then_inc(root_done, 1)

        def rows_vector(dve, steps, out, n, tokens, done):
            dve.wait_ge(sums_ps, done)
            steps.mark(nc.vector.tensor_tensor(turned[:, 0:n], partner[:, 0:n], rope[:, 1, tokens:tokens + n], ALU.mult))
            steps.link(dve, nc.vector.tensor_tensor(out, scaled[:, 0:n], rope[:, 0, tokens:tokens + n], ALU.mult))
            dve.wait_ge(root_done, done)
            steps.mark(nc.vector.reciprocal(root[:, 0:n], root[:, 0:n]))
            steps.link(dve, nc.vector.tensor_tensor(out, out, turned[:, 0:n], ALU.add))
            nc.vector.tensor_tensor(out, out, root[:, 0:n], ALU.mult).then_inc(rows_done, 1)

        with nc.Block() as block:

            @block.sync
            def _(sp):
                front_sync(sp)
                sp.dma_start(gains[:], a["gains"]).then_inc(const_in, 16)
                sp.dma_start(rot[:], a["rot"]).then_inc(const_in, 16)
                sp.dma_start(rope[:], a["rope"]).then_inc(const_in, 16)
                sp.dma_start(wk[:], a["attn_wk"]).then_inc(k_in, 16)
                sp.dma_start(wv[:], a["attn_wv"]).then_inc(v_in, 16)
                with sp.Fori(0, HEADS // 2) as i:
                    for u in range(2):
                        sp.wait_ge(proj_ps, i * 2 + (u + KEY_ROWS - 1))
                        sp.dma_start(wq[u][:], a["attn_wq"][ds(i * 2 + u, 1)].rearrange("h p k n -> (h p) k n")).then_inc(wq_in[u], 16)

            @block.gpsimd
            def _(pool):
                pool.sem_inc(o_stored, 2)
                with pool.Fori(0, HEADS // 2) as i:
                    for u in range(2):
                        pool.wait_ge(o_copied, i * 2 + (u + 2))
                        pool.dma_start(mixed[ds(i * (2 * HD) + u * HD, HD), 0:SEQ], o[u][:]).then_inc(o_out, 16)
                        pool.wait_ge(o_out, i * 32 + (16 * u + 16))
                        pool.sem_inc(o_stored, 1)

            @block.tensor
            def _(pe):
                def transpose_tile(head, q):
                    tile = head * QT + q
                    pe.wait_ge(norm_done, tile + 1)
                    pe.wait_ge(pT_copied, tile + 1)
                    for t in range(TILES):
                        last = nc.tensor.transpose(ps[:, 4 + t // 4, (t % 4) * P:(t % 4 + 1) * P], p[q % 2][:, t * P:(t + 1) * P], ident)
                    last.then_inc(pT_ps, 1)

                pe.sem_inc(pT_ps, 2)
                pe.sem_inc(o_ps, 1)
                front_tensor(pe)
                pe.wait_ge(hT_done, hT_all)
                pe.wait_ge(v_in, 16)
                for t in range(TILES):
                    if t >= 2:
                        pe.wait_ge(v_copied, t - 1)
                    for k in range(KC):
                        last = nc.tensor.matmul(ps[:, t % 2, 0:KV * HD], hT[:, k, t * P:(t + 1) * P], wv[:, k, :],
                                                start=k == 0, stop=k == KC - 1)
                    last.then_inc(v_ps, 1)
                pe.wait_ge(k_in, 16)
                pe.wait_ge(const_in, 48)
                pe.wait_ge(ones_done, 2)
                done = 0
                for n_kv in range(KV):
                    for tokens, n in key_parts:
                        if done:
                            pe.wait_ge(rows_done, done)
                        done += 1
                        rows_tensor(pe, lambda k: wk[:, k, n_kv * HD:(n_kv + 1) * HD], n, tokens, done)
                pe.wait_ge(v_copied, TILES)
                for n_kv in range(KV):
                    with pe.Fori(0, PER_KV // 2) as i:
                        for u in range(2):
                            head = i * 2 + (n_kv * PER_KV + u)
                            pe.wait_ge(wq_in[u], i * 16 + (n_kv * PER_KV // 2 * 16 + 16))
                            pe.wait_ge(rows_done, head + KEY_ROWS)
                            pe.wait_ge(o_copied, head + 1)
                            rows_tensor(pe, lambda k: wq[u][:, k, :], SEQ, CTX, head + (KEY_ROWS + 1))
                            pe.wait_ge(rows_done, head + (KEY_ROWS + 1))
                            for q in range(QT):
                                pe.wait_ge(p_done, head * QT + (q + 1))
                                for tokens, n in key_parts:
                                    last = nc.tensor.matmul(ps[:, 2 * (q % 2) + tokens // HALF, 0:n], qT[u][:, q * P:(q + 1) * P],
                                                            kT[n_kv][:, tokens:tokens + n], start=True, stop=True)
                                last.then_inc(s_ps, 1)
                                if q:
                                    transpose_tile(head, q - 1)
                            transpose_tile(head, QT - 1)
                            pe.wait_ge(pT_copied, head * QT + (QT + 1))
                            for t in range(TILES):
                                last = nc.tensor.matmul(proj[:], v[:, t, n_kv * HD:(n_kv + 1) * HD], pT[:, t, :],
                                                        start=t == 0, stop=t == TILES - 1)
                            last.then_inc(o_ps, 1)

            @block.scalar
            def _(act):
                def copy_tile(head, q):
                    act.wait_ge(pT_ps, head * QT + (q + 3))
                    act.wait_ge(o_ps, head + 1)
                    nc.scalar.copy(pT[:, :, q * P:(q + 1) * P],
                                   ps[:, 4:6, :].rearrange("p b (t c) -> p (b t) c", c=P)[:, 0:TILES, :]).then_inc(pT_copied, 1)

                act.sem_inc(p_done, 2)
                act.sem_inc(pT_copied, 1)
                act.sem_inc(o_copied, 1)
                front_scalar(act)
                for t in range(TILES):
                    act.wait_ge(v_ps, t + 1)
                    nc.scalar.copy(v[:, t, :], ps[:, t % 2, 0:KV * HD]).then_inc(v_copied, 1)
                act.wait_ge(const_in, 48)
                act.wait_ge(ones_done, 2)
                for done in range(KEY_ROWS):
                    rows_scalar(act, 1, key_parts[done % 2][1], done + 1)
                with act.Fori(0, HEADS // 2) as i:
                    for u in range(2):
                        head = i * 2 + u
                        rows_scalar(act, 0, SEQ, head + (KEY_ROWS + 1))
                        for q in range(QT):
                            tile = head * QT + q
                            act.wait_ge(max_done, tile + 1)
                            act.wait_ge(pT_ps, tile + 1)
                            b = 2 * (q % 2)
                            nc.scalar.activation(p[q % 2][:], ps[:, b:b + 2, :].rearrange("p b n -> p (b n)")[:, 0:TOK], ACT.Exp,
                                                 bias=neg_max[:, q % 2:q % 2 + 1], scale=SCALE,
                                                 accum_out=total[:, q % 2:q % 2 + 1]).then_inc(p_done, 1)
                            if q:
                                copy_tile(head, q - 1)
                        copy_tile(head, QT - 1)
                        act.wait_ge(o_ps, head + 2)
                        act.wait_ge(o_stored, head + 1)
                        nc.scalar.copy(o[u][:], proj[:]).then_inc(o_copied, 1)

            @block.vector
            def _(dve):
                nc.vector.memset(ones[:], 1.0).then_inc(ones_done, 1)
                nc.vector.memset(eps[:], EPS).then_inc(ones_done, 1)
                front_vector(dve)
                dve.wait_ge(const_in, 48)
                steps = Counter(step)
                done = 0
                for n_kv in range(KV):
                    for tokens, n in key_parts:
                        done += 1
                        rows_vector(dve, steps, kT[n_kv][:, tokens:tokens + n], n, tokens, done)

                def norm_tile(head, q):
                    at = slice(q % 2, q % 2 + 1)
                    dve.wait_ge(p_done, head * QT + (q + 3))
                    steps.link(dve, nc.vector.reciprocal(inv[:, at], total[:, at]))
                    nc.vector.tensor_scalar(p[q % 2][:], p[q % 2][:], inv[:, at], None, ALU.mult).then_inc(norm_done, 1)

                with dve.Fori(0, HEADS // 2) as i:
                    steps.loop(i, 2 * HEAD_STEPS)
                    for u in range(2):
                        head = i * 2 + u
                        rows_vector(dve, steps, qT[u][:], SEQ, CTX, head + (KEY_ROWS + 1))
                        for q in range(QT):
                            b = 2 * (q % 2)
                            dve.wait_ge(s_ps, head * QT + (q + 1))
                            steps.link(dve, nc.vector.tensor_reduce(biggest[:, q % 2:q % 2 + 1], ps[:, b:b + 2, :].rearrange("p b n -> p (b n)")[:, 0:TOK],
                                                                    AX_X, ALU.max))
                            nc.vector.tensor_scalar(neg_max[:, q % 2:q % 2 + 1], biggest[:, q % 2:q % 2 + 1], -SCALE, None, ALU.mult).then_inc(max_done, 1)
                            if q:
                                norm_tile(head, q - 1)
                        norm_tile(head, QT - 1)
                steps.end(HEADS // 2)


def token_stages(layer):
    if layer == 0:
        return TILES, 0, ((0, 1, CON), (1, 2, LAT))
    return TILES - CTX_TILES, CTX_TILES, ((0, 2, LAT),)


NORM_STEPS = 7


def post_norm(nc, dve, steps, x_tile, update, gain, r, stats, mv, ln, read_done, var_done, root_done):
    nc.vector.tensor_tensor(r, update, gain, ALU.mult).then_inc(read_done[0], 1)
    dve.wait_ge(*read_done)
    steps.link(dve, nc.vector.scalar_tensor_tensor(r, x_tile, ALPHA, r, ALU.mult, ALU.add))
    for n in range(2):
        steps.mark(nc.vector.bn_stats(stats[:, n, :], r[:, n * HALF:(n + 1) * HALF]))
    steps.wait(dve)
    nc.vector.memset(mv[:, 2:3], EPS)
    steps.link(dve, nc.vector.bn_aggr(mv[:, 0:2], stats[:].rearrange("p a b -> p (a b)")))
    nc.vector.tensor_tensor(mv[:, 2:3], mv[:, 1:2], mv[:, 2:3], ALU.add).then_inc(var_done, 1)
    dve.wait_ge(*root_done)
    steps.link(dve, nc.vector.reciprocal(mv[:, 4:5], mv[:, 3:4]))
    steps.link(dve, nc.vector.tensor_scalar(r, r, mv[:, 0:1], mv[:, 4:5], ALU.subtract, ALU.mult))
    steps.link(dve, nc.vector.tensor_tensor(r, r, ln[:, 0, :], ALU.mult))
    return nc.vector.tensor_tensor(x_tile, r, ln[:, 1, :], ALU.add)


def post_mixer(nc, a, mod, mixed, h2, scores, x, ident, layer):
    T, x_first, streams = token_stages(layer)
    w_out = a["lru_w_out"] if layer == 0 else a["attn_w_out"]
    CH = w_out.shape[0] // P
    src = mixed.rearrange("(k p) n -> p k n", p=P)
    dst = scores[0:T * PH].rearrange("(t h) p s k -> h s p t k", h=PH)
    halves = [(at, min(HALF, T * P - at)) for at in range(0, T * P, HALF)]
    with Stage(nc, f"post{layer}") as s:
        ps = s.ps("ps", [P, 8, HALF])
        wo = s.sb("wo", [P, CH, D])
        mt = [s.sb(f"mt{u}", [P, CH, P]) for u in range(2)]
        rows = s.sb("rows", [P, 2, 3, D])
        ln = s.sb("ln", [P, 2, D])
        r = s.sb("r", [P, D])
        stats = s.sb("stats", [P, 2, 6])
        mv = s.sb("mv", [P, 5])
        h2b = [s.sb(f"h2b{u}", [P, D]) for u in range(2)]
        h2T = s.sb("h2T", [P, KC, T * P])
        wq = [s.sb(f"wq{u}", [P, KC, P]) for u in range(2)]
        keys = s.sb("keys", [P, 2, NK])
        qT = [s.sb(f"qT{u}", [P, T * P]) for u in range(2)]
        sb = [s.sb(f"sb{u}", [P, T, NK]) for u in range(2)]
        wo_in, rows_in, keys_in = (s.sem(n) for n in ("wo_in", "rows_in", "keys_in"))
        h2_out, s_out, wrap_out = (s.pool_dma_sem(n) for n in ("h2_out", "s_out", "wrap_out"))
        mt_in, wq_in = ([s.sem(f"{n}{u}") for u in range(2)] for n in ("mt_in", "wq_in"))
        step, var_done, root_done, h2_ready, h2T_ps = (
            s.sem(n) for n in ("step", "var_done", "root_done", "h2_ready", "h2T_ps"))
        y_ps, y_read, h2_stored, h2T_done, q_ps, q_copied, s_ps, s_copied, s_stored = (
            s.sem(n) for n in ("y_ps", "y_read", "h2_stored", "h2T_done", "q_ps", "q_copied", "s_ps", "s_copied", "s_stored"))
        with nc.Block() as block:

            @block.sync
            def _(sp):
                sp.dma_start(wo[:], w_out.rearrange("(k p) n -> p k n", p=P)).then_inc(wo_in, 16)
                n_rows = 0
                for c in sorted({c for _, _, c in streams}):
                    for j, kind in enumerate((G1, SC2, SH2)):
                        sp.dma_start(rows[:, c, j, :], mod_row(mod, layer, c, kind)).then_inc(rows_in, 16)
                        n_rows += 16
                sp.dma_start(ln[:, 0, :], row_of(a["ln_g"][layer, 0])).then_inc(rows_in, 16)
                sp.dma_start(ln[:, 1, :], row_of(a["ln_b"][layer, 0])).then_inc(rows_in, 16)
                with sp.Fori(0, T // 2) as i:
                    for u in range(2):
                        sp.wait_ge(y_ps, i * 2 + (u + 1))
                        sp.dma_start(mt[u][:], src[:, 0:CH, ds(i * (2 * P) + u * P, P)]).then_inc(mt_in[u], 16)
                sp.dma_start(keys[:], a["sub_keys"][layer]).then_inc(keys_in, 16)
                with sp.Fori(0, PH) as i:
                    for u in range(2):
                        sp.wait_ge(q_ps, i * 2 + (u + 1))
                        sp.dma_start(wq[u][:], a["peer_wq"][layer, ds(i * 2 + u, 1)].rearrange("h p k n -> (h p) k n")).then_inc(wq_in[u], 16)

            @block.gpsimd
            def _(pool):
                pool.sem_inc(h2_stored, 2)
                pool.sem_inc(s_stored, 2)
                with pool.Fori(0, T // 2) as i:
                    for u in range(2):
                        pool.wait_ge(h2_ready, i * 2 + (u + 1))
                        pool.dma_start(h2[ds(i * 2 + u, 1)].rearrange("t p d -> (t p) d"), h2b[u][:]).then_inc(h2_out, 16)
                        pool.wait_ge(h2_out, i * 32 + (16 * u + 16))
                        pool.sem_inc(h2_stored, 1)
                with pool.Fori(0, PH) as i:
                    for u in range(2):
                        pool.wait_ge(s_copied, i * 2 + (u + 3))
                        pool.dma_start(dst[ds(i, 1), u].rearrange("h p t k -> (h p) t k"), sb[u][:]).then_inc(s_out, 16)
                        pool.wait_ge(s_out, i * 32 + (16 * u + 16))
                        pool.sem_inc(s_stored, 1)
                pool.dma_start(scores[T * PH:T * PH + 2], scores[0:2]).then_inc(wrap_out, 16)
                pool.wait_ge(wrap_out, 16)

            @block.tensor
            def _(pe):
                pe.sem_inc(y_ps, 2)
                pe.sem_inc(q_ps, 2)
                pe.sem_inc(s_ps, 2)
                pe.wait_ge(wo_in, 16)
                with pe.Fori(0, T // 2) as i:
                    for u in range(2):
                        pe.wait_ge(mt_in[u], i * 16 + 16)
                        pe.wait_ge(y_read, i * 2 + (u + 1))
                        for h in range(2):
                            for k in range(CH):
                                last = nc.tensor.matmul(ps[:, 2 * u + h, :], mt[u][:, k, :], wo[:, k, h * HALF:(h + 1) * HALF],
                                                        start=k == 0, stop=k == CH - 1)
                        last.then_inc(y_ps, 1)
                    for u in range(2):
                        pe.wait_ge(h2_ready, i * 2 + (u + 1))
                        pe.wait_ge(h2T_done, i * 2 + (u + 1))
                        for k in range(KC):
                            last = nc.tensor.transpose(ps[:, 4 + 2 * u + k // 4, (k % 4) * P:(k % 4 + 1) * P],
                                                       h2b[u][:, k * P:(k + 1) * P], ident)
                        last.then_inc(h2T_ps, 1)
                pe.wait_ge(h2T_done, T + 2)
                pe.wait_ge(y_read, T + 2)
                pe.wait_ge(keys_in, 16)
                with pe.Fori(0, PH) as i:
                    for u in range(2):
                        pe.wait_ge(wq_in[u], i * 16 + 16)
                        pe.wait_ge(q_copied, i * 2 + (u + 1))
                        for h, (at, n) in enumerate(halves):
                            for k in range(KC):
                                last = nc.tensor.matmul(ps[:, 2 * u + h, 0:n], wq[u][:, k, :], h2T[:, k, at:at + n],
                                                        start=k == 0, stop=k == KC - 1)
                        last.then_inc(q_ps, 1)
                    for u in range(2):
                        pe.wait_ge(q_copied, i * 2 + (u + 3))
                        pe.wait_ge(s_copied, i * 2 + (u + 1))
                        for t in range(T):
                            last = nc.tensor.matmul(ps[:, 4 + 2 * u + t // 4, (t % 4) * P:(t % 4 + 1) * P],
                                                    qT[u][:, t * P:(t + 1) * P], keys[:, u, :], start=True, stop=True)
                        last.then_inc(s_ps, 1)

            @block.scalar
            def _(act):
                act.sem_inc(h2T_done, 2)
                act.sem_inc(q_copied, 2)
                with act.Fori(0, T // 2) as i:
                    for u in range(2):
                        act.wait_ge(var_done, i * 2 + (u + 1))
                        nc.scalar.activation(mv[:, 3:4], mv[:, 2:3], ACT.Sqrt).then_inc(root_done, 1)
                    for u in range(2):
                        act.wait_ge(h2T_ps, i * 2 + (u + 1))
                        nc.scalar.copy(h2T[:, :, ds(i * (2 * P) + u * P, P)],
                                       ps[:, 4 + 2 * u:6 + 2 * u, :].rearrange("p b (k c) -> p (b k) c", c=P)).then_inc(h2T_done, 1)
                with act.Fori(0, PH) as i:
                    for u in range(2):
                        act.wait_ge(q_ps, i * 2 + (u + 3))
                        act.wait_ge(s_ps, i * 2 + (u + 1))
                        nc.scalar.copy(qT[u][:], ps[:, 2 * u:2 * u + 2, :].rearrange("p b n -> p (b n)")[:, 0:T * P]).then_inc(q_copied, 1)

            @block.vector
            def _(dve):
                dve.sem_inc(y_read, 2)
                dve.sem_inc(s_copied, 2)
                dve.wait_ge(rows_in, 16 * (3 * len(streams) + 2))
                steps = Counter(step)
                for first, pairs, cond in streams:
                    with dve.Fori(0, pairs) as i:
                        steps.loop(i, 2 * (NORM_STEPS + 2))
                        for u in range(2):
                            t = i * 2 + (2 * first + u)
                            dve.wait_ge(y_ps, t + 3)
                            xt = x[:, ds(t + x_first, 1), :].rearrange("p a d -> p (a d)")
                            steps.link(dve, post_norm(nc, dve, steps, xt, ps[:, 2 * u:2 * u + 2, :].rearrange("p b n -> p (b n)"),
                                                      rows[:, cond, 0, :], r[:], stats, mv, ln, (y_read, t + 3), var_done,
                                                      (root_done, t + 1)))
                            dve.wait_ge(h2_stored, t + 1)
                            dve.wait_ge(h2T_done, t + 1)
                            steps.link(dve, nc.vector.tensor_tensor(h2b[u][:], xt, rows[:, cond, 1, :], ALU.mult))
                            nc.vector.tensor_tensor(h2b[u][:], h2b[u][:], rows[:, cond, 2, :], ALU.add).then_inc(h2_ready, 1)
                    steps.end(pairs)
                with dve.Fori(0, PH) as i:
                    for u in range(2):
                        dve.wait_ge(s_ps, i * 2 + (u + 3))
                        dve.wait_ge(s_stored, i * 2 + (u + 1))
                        nc.vector.tensor_copy(sb[u][:].rearrange("p t k -> p (t k)"),
                                              ps[:, 4 + 2 * u:6 + 2 * u, :].rearrange("p b n -> p (b n)")[:, 0:T * P]).then_inc(s_copied, 1)


def top16(nc, dve, steps, values, rest, top, at, hold):
    hold()
    steps.link(dve, nc.vector.max(top[:, 0:8], values))
    hold()
    steps.mark(nc.vector.max_index(at[:, 0:8], top[:, 0:8], values))
    steps.link(dve, nc.vector.match_replace(rest, top[:, 0:8], values, LOWEST))
    hold()
    steps.link(dve, nc.vector.max(top[:, 8:16], rest))
    hold()
    steps.link(dve, nc.vector.max_index(at[:, 8:16], top[:, 8:16], rest))


ROUTE_STEPS = 26


def peer(nc, a, mod, h2, scores, x, layer, out):
    T, x_first, streams = token_stages(layer)
    N = T * PH
    NJ = TOPK // BATCH
    conds = sorted({c for _, _, c in streams})
    with Stage(nc, f"peer{layer}") as s:
        acc = s.ps("acc", [P, 2, HALF])
        ring = s.sb("ring", [P, TOPK, ROW])
        h2b = [s.sb(f"h2b{u}", [P, D]) for u in range(2)]
        product = [s.sb(f"product{n}", [P, D]) for n in range(2)]
        diag = s.sb("diag", [P, TOPK, P])
        eye = s.sb("eye", [P, P])
        zero = s.sb("zero", [1, HALF], mybir.dt.bfloat16)
        g2 = s.sb("g2", [P, 2, D])
        ln = s.sb("ln", [P, 2, D])
        iota = s.sb("iota", [P, TOPK])
        stats, mv = s.sb("stats", [P, 2, 6]), s.sb("mv", [P, 5])
        scb = [s.sb(f"scb{u}", [P, 2, NK]) for u in range(2)]
        rest = s.sb("rest", [P, NK])
        cand, cand_rest = (s.sb(n, [P, TOPK * TOPK]) for n in ("cand", "cand_rest"))
        hot = s.sb("hot", [P, TOPK, TOPK])
        top = [s.sb(f"top{n}", [P, TOPK]) for n in range(3)]
        at = [s.sb(f"at{n}", [P, TOPK], U32) for n in range(3)]
        place, key = s.sb("place", [P, TOPK], U32), [s.sb(f"key{n}", [P, TOPK]) for n in range(2)]
        idx = [s.sb(f"idx{u}", [P, TOPK], U32) for u in range(2)]
        neg_max, total, inv = (s.sb(n, [P, 2]) for n in ("neg_max", "total", "inv"))
        expo, share, dots, gelu, weight = ([s.sb(f"{n}{u}", [P, TOPK]) for u in range(2)]
                                           for n in ("expo", "share", "dots", "gelu", "weight"))
        const_in, zero_done, idx_done, max_done, exp_done, step, sc_used = (
            s.sem(n) for n in ("const_in", "zero_done", "idx_done", "max_done", "exp_done", "step", "sc_used"))
        gelu_done, weight_done, diag_done, tile_ps, var_done, root_done, x_out = (
            s.sem(n) for n in ("gelu_done", "weight_done", "diag_done", "tile_ps", "var_done", "root_done", "x_out"))
        held, slots_granted = s.sem("held"), s.sem("slots_granted")
        row_in = [s.pool_dma_sem(f"row_in{k}") for k in range(TOPK)]
        sc_in = [s.sem(f"sc_in{u}") for u in range(2)]
        h2_in = [s.sem(f"h2_in{u}") for u in range(2)]
        row_used, dot_done, acc_read, x_done = (s.sem(n) for n in ("row_used", "dot_done", "acc_read", "x_done"))

        def tiles(eng):
            for first, pairs, cond in streams:
                with eng.Fori(0, pairs) as i:
                    for tu in range(2):
                        yield cond, tu, i * 2 + (2 * first + tu), i + first

        with nc.Block() as block:

            @block.sync
            def _(sp):
                for u in range(2):
                    sp.dma_start(scb[u][:], scores[u]).then_inc(sc_in[u], 16)
                sp.dma_start(iota[:], a["iota"].rearrange("(a n) -> a n", a=1).broadcast_to([P, TOPK])).then_inc(const_in, 16)
                sp.dma_start(eye[:], a["eye"]).then_inc(const_in, 16)
                for c in conds:
                    sp.dma_start(g2[:, c, :], mod_row(mod, layer, c, G2)).then_inc(const_in, 16)
                sp.dma_start(ln[:, 0, :], row_of(a["ln_g"][layer, 1])).then_inc(const_in, 16)
                sp.dma_start(ln[:, 1, :], row_of(a["ln_b"][layer, 1])).then_inc(const_in, 16)
                for cond, tu, t, _ in tiles(sp):
                    sp.wait_ge(x_done, t + 1)
                    sp.dma_start(h2b[tu][:], h2[ds(t, 1)].rearrange("t p d -> (t p) d")).then_inc(h2_in[tu], 16)
                    with sp.Fori(0, PH // 2) as i:
                        for u in range(2):
                            sp.wait_ge(sc_used, t * PH + i * 2 + (u + 1))
                            sp.dma_start(scb[u][:], scores[ds(t * PH + i * 2 + (u + 2), 1)].rearrange("g p s k -> (g p) s k")).then_inc(sc_in[u], 16)

            @block.gpsimd
            def _(pool):
                with pool.Fori(0, N // 2) as i:
                    for u in range(2):
                        pool.wait_ge(idx_done, i * 2 + (u + 1))
                        for k in range(TOPK):
                            if k % BATCH == 0:
                                pool.wait_ge(row_used, i * (2 * TOPK) + (u * TOPK + k + BATCH))
                                pool.sem_inc(slots_granted, 1)
                            pool.indirect_dma_start(
                                out=ring[:, k, :], out_offset=None, in_=a["uv"],
                                in_offset=bass.IndirectOffsetOnAxis(ap=idx[u][:, k:k + 1], axis=0)).then_inc(row_in[k], 16)

            @block.vector
            def _(dve):
                dve.sem_inc(dot_done, 2)
                dve.sem_inc(acc_read, 1)
                dve.sem_inc(x_done, 2)
                nc.vector.memset(zero[:], 0.0).then_inc(zero_done, 1)
                steps = Counter(step)
                n_const = 16 * (4 + len(conds))

                def hold():
                    dve.sem_inc(held, 1)

                def route_half(u, n):
                    top16(nc, dve, steps, scb[u][:, n, :], rest[:], top[n][:], at[n][:], hold)

                def route_pairs(u, g):
                    grid = [P, TOPK, TOPK]
                    nc.vector.tensor_tensor(cand[:].rearrange("p (a b) -> p a b", b=TOPK),
                                            top[0][:].unsqueeze(2).broadcast_to(grid),
                                            top[1][:].unsqueeze(1).broadcast_to(grid), ALU.add).then_inc(sc_used, 1)
                    dve.wait_ge(sc_used, g + 1)
                    top16(nc, dve, steps, cand[:], cand_rest[:], top[2][:], at[2][:], hold)
                    nc.vector.tensor_scalar(neg_max[:, u:u + 1], top[2][:, 0:1], -1.0, None, ALU.mult).then_inc(max_done, 1)

                def route_experts(u):
                    grid = [P, TOPK, TOPK]
                    for n, (op, by) in enumerate(((ALU.logical_shift_right, 4), (ALU.bitwise_and, TOPK - 1))):
                        steps.link(dve, nc.vector.tensor_scalar(place[:], at[2][:], by, None, op))
                        steps.link(dve, nc.vector.tensor_tensor(hot[:], place[:].unsqueeze(2).broadcast_to(grid),
                                                                iota[:].unsqueeze(1).broadcast_to(grid), ALU.is_equal))
                        steps.link(dve, nc.vector.tensor_tensor(hot[:], hot[:], at[n][:].unsqueeze(1).broadcast_to(grid), ALU.mult))
                        steps.link(dve, nc.vector.tensor_reduce(key[n][:], hot[:], AX_X, ALU.add))
                    steps.link(dve, nc.vector.tensor_scalar(key[0][:], key[0][:], float(NK), float(layer * EXPERTS), ALU.mult, ALU.add))
                    nc.vector.tensor_tensor(idx[u][:], key[0][:], key[1][:], ALU.add).then_inc(idx_done, 1)

                def route_share(u, g):
                    dve.wait_ge(exp_done, g + 1)
                    steps.link(dve, nc.vector.reciprocal(inv[:, u:u + 1], total[:, u:u + 1]))
                    steps.link(dve, nc.vector.tensor_scalar(share[u][:], expo[u][:], inv[:, u:u + 1], None, ALU.mult))

                def dot_batch(u, tu, g, j):
                    for k in range(j * BATCH, (j + 1) * BATCH):
                        dve.wait_ge(row_in[k], (g + 1) * 16)
                        dve.wait_ge(dot_done, g * TOPK + (k + 1))
                        nc.vector.scalar_tensor_tensor(product[k % 2][:], ring[:, k, 0:D], 1.0, h2b[tu][:], ALU.mult, ALU.mult,
                                                       accum_out=dots[u][:, k:k + 1]).then_inc(dot_done, 1)

                def weigh_batch(u, g, j):
                    dve.wait_ge(gelu_done, g * NJ + (j + 1))
                    part = slice(j * BATCH, (j + 1) * BATCH)
                    nc.vector.tensor_tensor(weight[u][:, part], gelu[u][:, part], share[u][:, part], ALU.mult).then_inc(weight_done, 1)

                dve.wait_ge(const_in, n_const)
                for u in range(2):
                    dve.wait_ge(sc_in[u], 16)
                    route_half(u, 0)
                    route_half(u, 1)
                    route_pairs(u, u)
                    route_experts(u)
                    route_share(u, u)
                for cond, tu, t, pair in tiles(dve):
                    dve.wait_ge(h2_in[tu], pair * 16 + 16)
                    hold()
                    with dve.Fori(0, PH // 2) as i:
                        for u in range(2):
                            g = t * PH + i * 2 + u
                            steps.base, steps.n = g * ROUTE_STEPS + 2 * ROUTE_STEPS + t * NORM_STEPS, 0
                            dot_batch(u, tu, g, 0)
                            dve.wait_ge(sc_in[u], t * (PH // 2 * 16) + i * 16 + 32)
                            route_half(u, 0)
                            dot_batch(u, tu, g, 1)
                            weigh_batch(u, g, 0)
                            route_half(u, 1)
                            dot_batch(u, tu, g, 2)
                            weigh_batch(u, g, 1)
                            route_pairs(u, g + 2)
                            dot_batch(u, tu, g, 3)
                            weigh_batch(u, g, 2)
                            route_experts(u)
                            weigh_batch(u, g, 3)
                            route_share(u, g + 2)
                            assert steps.n == ROUTE_STEPS
                        hold()
                    steps.base, steps.n = (t + 1) * (PH * ROUTE_STEPS) + 2 * ROUTE_STEPS + t * NORM_STEPS, 0
                    dve.wait_ge(tile_ps, t + 1)
                    xt = x[:, ds(t + x_first, 1), :].rearrange("p a d -> p (a d)")
                    post_norm(nc, dve, steps, xt, acc[:].rearrange("p b n -> p (b n)"), g2[:, cond, :], product[0][:], stats,
                              mv, ln, (acc_read, t + 2), var_done, (root_done, t + 1)).then_inc(x_done, 1)
                    dve.wait_ge(x_done, t + 3)
                    hold()

            @block.scalar
            def _(act):
                def exponentials(u, g):
                    act.wait_ge(max_done, g + 1)
                    nc.scalar.activation(expo[u][:], top[2][:], ACT.Exp, bias=neg_max[:, u:u + 1],
                                         accum_out=total[:, u:u + 1]).then_inc(exp_done, 1)

                def gelu_batch(u, g, j):
                    act.wait_ge(dot_done, g * TOPK + ((j + 1) * BATCH + 2))
                    part = slice(j * BATCH, (j + 1) * BATCH)
                    nc.scalar.activation(gelu[u][:, part], dots[u][:, part], ACT.Gelu).then_inc(gelu_done, 1)

                def diag_batch(u, g, j):
                    act.wait_ge(weight_done, g * NJ + (j + 1))
                    act.wait_ge(row_used, g * TOPK + (j + 1) * BATCH)
                    for k in range(j * BATCH, (j + 1) * BATCH):
                        last = nc.scalar.mul(diag[:, k, :], eye[:], weight[u][:, k:k + 1])
                    last.then_inc(diag_done, 1)

                for u in range(2):
                    exponentials(u, u)
                for cond, tu, t, _ in tiles(act):
                    with act.Fori(0, PH // 2) as i:
                        for u in range(2):
                            g = t * PH + i * 2 + u
                            gelu_batch(u, g, 0)
                            gelu_batch(u, g, 1)
                            diag_batch(u, g, 0)
                            gelu_batch(u, g, 2)
                            diag_batch(u, g, 1)
                            exponentials(u, g + 2)
                            gelu_batch(u, g, 3)
                            diag_batch(u, g, 2)
                            diag_batch(u, g, 3)
                    act.wait_ge(var_done, t + 1)
                    nc.scalar.activation(mv[:, 3:4], mv[:, 2:3], ACT.Sqrt).then_inc(root_done, 1)
                    if out is not None:
                        act.wait_ge(x_done, t + 3)
                        xt = x[:, ds(t + x_first, 1), :].rearrange("p a d -> p (a d)")
                        act.dma_start(out[ds(t * P, P), :], xt).then_inc(x_out, 16)
                if out is not None:
                    act.wait_ge(x_out, 16 * T)

            @block.tensor
            def _(pe):
                pe.sem_inc(row_used, TOPK)
                pe.wait_ge(zero_done, 1)
                for cond, tu, t, _ in tiles(pe):
                    pe.wait_ge(acc_read, t + 1)
                    for h in range(2):
                        nc.tensor.matmul(acc[:, h, :], zero[:, 0:P], zero[:], start=True, stop=False)
                    with pe.Fori(0, PH // 2) as i:
                        for u in range(2):
                            for j in range(NJ):
                                pe.wait_ge(diag_done, t * (PH * NJ) + i * (2 * NJ) + (u * NJ + j + 1))
                                for k in range(j * BATCH, (j + 1) * BATCH):
                                    for h in range(2):
                                        last = nc.tensor.matmul(acc[:, h, :], diag[:, k, :],
                                                                ring[:, k, D + h * HALF:D + (h + 1) * HALF],
                                                                start=False, stop=False)
                                    last.then_inc(row_used, 1)
                    for h in range(2):
                        last = nc.tensor.matmul(acc[:, h, :], zero[:, 0:P], zero[:], start=False, stop=True)
                    last.then_inc(tile_ps, 1)



_OUT = ("out_dram", (1, SEQ, D))


def layout(i):
    c = np.ascontiguousarray
    cond = np.stack([i["c"][0], i["c_ctx"]], -1).reshape(KC, P, 2).transpose(1, 0, 2)
    w_in = i["lru_w_in"][0].reshape(KC, P, 2, NB, LB).transpose(3, 1, 0, 2, 4).reshape(NB, P, KC, 2 * LB)
    gate_w = i["lru_gate_w"][0].transpose(1, 2, 0, 3)
    gb = i["lru_gate_b"][0].reshape(2, NB, 2, LB).transpose(3, 1, 0, 2).reshape(LB, NB, 4)
    lru_cols = np.concatenate([
        i["lru_conv_w"][0].reshape(TAPS, NB, LB).transpose(2, 1, 0),
        i["lru_conv_b"][0].reshape(1, NB, LB).transpose(2, 1, 0),
        gb,
        i["lru_lambda"][0].reshape(2, NB, LB).transpose(2, 1, 0)], -1)
    uv = np.concatenate([i["peer_u"], i["peer_v"]], -1).reshape(DEPTH * EXPERTS, ROW)
    wq = i["peer_w_q"].reshape(DEPTH, KC, P, 2 * PH, P).transpose(0, 3, 2, 1, 4)
    qkv = i["attn_w_qkv"][0]
    n_q = HEADS * HD
    attn_wq = qkv[:, :n_q].reshape(KC, P, HEADS, HD).transpose(2, 1, 0, 3)
    attn_wk = qkv[:, n_q:n_q + KV * HD].reshape(KC, P, KV * HD).transpose(1, 0, 2)
    attn_wv = qkv[:, n_q + KV * HD:].reshape(KC, P, KV * HD).transpose(1, 0, 2)
    gains = np.stack([i["attn_q_gain"][0], i["attn_k_gain"][0]], -1)
    return {k: c(v) for k, v in {
        "x": i["x"][0], "ctx": i["ctx"][0], "cond": cond, "mod_w": i["mod_w"], "mod_b": i["mod_b"],
        "ln_g": i["ln_g"], "ln_b": i["ln_b"], "w_in": w_in, "gate_w": gate_w, "lru_cols": lru_cols,
        "lru_w_out": i["lru_w_out"][0], "attn_wq": attn_wq, "attn_wk": attn_wk, "attn_wv": attn_wv,
        "gains": gains, "attn_w_out": i["attn_w_out"][0], "peer_wq": wq,
        "sub_keys": i["peer_sub_keys"].transpose(0, 3, 1, 2), "uv": uv,
        "rope": rope_tables(), "rot": rope_rotation(), "eye": np.eye(P, dtype=np.float32), "iota": np.arange(TOPK, dtype=np.float32)}.items()}


GRID_W = 64
ROPE_THETA = 10000.0


def rope_tables():
    axis = HD // 2
    token = np.arange(SEQ)
    place = np.stack([token // GRID_W, token % GRID_W]).astype(np.float32)
    freq = np.float32(ROPE_THETA) ** (-np.arange(0, axis, 2, dtype=np.float32) / np.float32(axis))
    angle = place[:, None, None, :] * freq[None, None, :, None]
    angle = np.broadcast_to(angle, (2, 2, axis // 2, SEQ)).reshape(HD, SEQ)
    out = np.zeros((HD, 2, TOK), np.float32)
    out[:, 0, :CTX] = 1.0
    out[:, 0, CTX:], out[:, 1, CTX:] = np.cos(angle), np.sin(angle)
    return out


def rope_rotation():
    half = HD // 4
    rot = np.zeros((HD, HD), np.float32)
    for axis in range(2):
        for n in range(half):
            one, two = axis * 2 * half + n, axis * 2 * half + half + n
            rot[two, one] = -1.0
            rot[one, two] = 1.0
    return rot


def program(nc, a, out, upto=99):
    mod = nc.dram_tensor("mod_scratch", (2, DEPTH * MOD), F32, kind="Internal").ap()
    mixed = nc.dram_tensor("mixed_scratch", (D_RNN, TOK), F32, kind="Internal").ap()
    h2 = nc.dram_tensor("h2_scratch", (TILES, P, D), F32, kind="Internal").ap()
    scores = nc.dram_tensor("score_scratch", (TILES * PH + 2, P, 2, NK), F32, kind="Internal").ap()
    with nc.sbuf_tensor("x_all", [P, TILES, D], F32) as x, nc.sbuf_tensor("eye_sb", [P, P], F32) as ident, \
            nc.semaphore("eye_in") as eye_in:
        with nc.Block() as block:

            @block.sync
            def _(sp):
                sp.dma_start(ident[:], a["eye"]).then_inc(eye_in, 16)
                sp.wait_ge(eye_in, 16)

        modulation(nc, a, mod)
        if upto >= 1:
            lru_mixer(nc, a, mod, mixed, x, ident[:])
        if upto >= 2:
            post_mixer(nc, a, mod, mixed, h2, scores, x, ident[:], 0)
        if upto >= 3:
            peer(nc, a, mod, h2, scores, x, 0, None)
        if upto >= 4:
            attn_mixer(nc, a, mod, mixed, x, ident[:])
        if upto >= 5:
            post_mixer(nc, a, mod, mixed, h2, scores, x, ident[:], 1)
        if upto >= 6:
            peer(nc, a, mod, h2, scores, x, 1, out)


def kernel(**inputs):
    import concourse.bacc as _bacc
    from concourse.bass_utils import run_bass_kernel_spmd as _run

    nc = _bacc.Bacc("TRN2", target_bir_lowering=False, num_devices=1)
    arrays, a = {}, {}
    for name, v in layout({k: np.asarray(v) for k, v in inputs.items()}).items():
        arrays[f"in_{name}"] = v
        a[name] = nc.dram_tensor(f"in_{name}", v.shape, F32, kind="ExternalInput").ap()
    name, shape = _OUT
    out = nc.dram_tensor(name, shape, F32, kind="ExternalOutput").ap()
    program(nc, a, out[0])
    r = _run(nc, [arrays], core_ids=[0])
    return r.results[0][name]
```

```python
from contextlib import ExitStack

import concourse.bass as bass
import numpy as np
from concourse import mybir

F32 = mybir.dt.float32
U32 = mybir.dt.uint32
ALU = mybir.AluOpType
ACT = mybir.ActivationFunctionType
AX_X = mybir.AxisListType.X
ds = bass.ds

P = 128
D = 1024
KC = D // P
CTX = 256
SEQ = 512
TOK = CTX + SEQ
TILES = TOK // P
CTX_TILES = CTX // P
DEPTH = 2
MOD = 6 * D
SH1, SC1, G1, SH2, SC2, G2 = range(6)
LAT, CON = 0, 1

D_RNN = 1280
LB = 80
LBP = 96
NB = D_RNN // LB
TAPS = 4
PAD_L, PAD_R = 2, 1
COLS = TAPS + 1 + 4 + 2
LRU_C = 8.0

HEADS = 8
KV = 2
HD = 128

PH = 8
NK = 128
TOPK = 16
EXPERTS = NK * NK
ROW = 2 * D
RING = 16
BATCH = 4

ALPHA = float((2 * DEPTH) ** 0.25)
EPS = 1e-6
LOWEST = -3.0e38

HALF = 512


class Counter:

    def __init__(self, sem):
        self.sem, self.base, self.n = sem, 0, 0

    def loop(self, i, per):
        self.start = self.base + self.n
        self.per = per
        self.base, self.n = self.start + i * per, 0

    def end(self, rounds):
        assert self.n == self.per, (self.n, self.per)
        self.base, self.n = self.start + rounds * self.per, 0

    def mark(self, ins):
        self.n += 1
        ins.then_inc(self.sem, 1)

    def wait(self, eng, back=0):
        eng.wait_ge(self.sem, self.base + (self.n - back))

    def link(self, eng, ins):
        self.n += 1
        ins.then_inc(self.sem, 1)
        eng.wait_ge(self.sem, self.base + self.n)


class Stage:

    def __init__(self, nc, name):
        self.nc, self.name, self.stack, self.sems = nc, name, ExitStack(), []

    def __enter__(self):
        self.stack.__enter__()
        return self

    def __exit__(self, *e):
        if e[0] is None:
            self.nc.clear_and_free_semaphores(self.sems)
            self.nc.all_engine_barrier()
        return self.stack.__exit__(*e)

    def sb(self, name, shape, dt=F32):
        return self.stack.enter_context(self.nc.sbuf_tensor(f"{self.name}_{name}", shape, dt))

    def ps(self, name, shape):
        return self.stack.enter_context(self.nc.psum_tensor(f"{self.name}_{name}", shape, F32))

    def sem(self, name):
        self.sems.append(self.nc.alloc_semaphore(f"{self.name}_{name}"))
        return self.sems[-1]

    def pool_dma_sem(self, name):
        return self.nc.alloc_semaphore(f"{self.name}_{name}")


class OutWeights(Stage):

    def __init__(self, nc, a, layer):
        super().__init__(nc, f"out{layer}")
        self.src = a["lru_w_out"] if layer == 0 else a["attn_w_out"]
        self.chunks = self.src.shape[0] // P

    def __enter__(self):
        super().__enter__()
        self.w = self.sb("w", [P, self.chunks, D])
        self.loaded = self.sem("loaded")
        return self

    def load(self, eng):
        eng.dma_start(self.w[:], self.src.rearrange("(k p) n -> p k n", p=P)).then_inc(self.loaded, 16)


def mod_row(mod, layer, cond, kind):
    at = layer * MOD + kind * D
    return mod[cond:cond + 1, at:at + D].broadcast_to([P, D])


def row_of(vector):
    return vector.rearrange("(a d) -> a d", a=1).broadcast_to([P, D])


def modulation(nc, a, mod):
    CH = MOD // HALF
    NBUF = 4
    w = a["mod_w"].rearrange("l (k p) n -> l p k n", p=P)
    with Stage(nc, "mod") as s:
        cond = s.sb("cond", [P, KC, 2])
        act = s.sb("act", [P, KC, 2])
        wbuf = [s.sb(f"w{u}", [P, KC, HALF]) for u in range(NBUF)]
        bias = s.sb("bias", [2, DEPTH * MOD])
        row = s.sb("row", [2, DEPTH * MOD])
        psum = s.ps("ps", [P, NBUF, HALF])
        cond_in, bias_in, silu_done, plus1 = (s.sem(n) for n in ("cond_in", "bias_in", "silu_done", "plus1"))
        w_in = [s.sem(f"w_in{u}") for u in range(NBUF)]
        mm_done, row_done = s.sem("mm_done"), s.sem("row_done")
        row_out = s.sem("row_out")
        with nc.Block() as block:

            @block.sync
            def _(sp):
                sp.dma_start(cond[:], a["cond"]).then_inc(cond_in, 16)
                sp.dma_start(bias[:], a["mod_b"].rearrange("l n -> (l n)").rearrange("(a n) -> a n", a=1)
                             .broadcast_to([2, DEPTH * MOD])).then_inc(bias_in, 16)
                for layer in range(DEPTH):
                    with sp.Fori(0, CH // NBUF) as i:
                        for u in range(NBUF):
                            sp.wait_ge(mm_done, i * NBUF + (layer * CH + u + 1))
                            sp.dma_start(wbuf[u][:], w[layer, :, :, ds((i * NBUF + u) * HALF, HALF)]).then_inc(w_in[u], 16)
                sp.wait_ge(row_done, NBUF + DEPTH * CH)
                sp.dma_start(mod, row[:]).then_inc(row_out, 16)
                sp.wait_ge(row_out, 16)

            @block.scalar
            def _(act_e):
                act_e.wait_ge(cond_in, 16)
                nc.scalar.activation(act[:], cond[:], ACT.Silu).then_inc(silu_done, 1)

            @block.tensor
            def _(pe):
                pe.sem_inc(mm_done, NBUF)
                pe.wait_ge(silu_done, 1)
                for layer in range(DEPTH):
                    with pe.Fori(0, CH // NBUF) as i:
                        for u in range(NBUF):
                            pe.wait_ge(w_in[u], (i + (layer * (CH // NBUF) + 1)) * 16)
                            pe.wait_ge(row_done, i * NBUF + (layer * CH + u + 1))
                            for k in range(KC):
                                last = nc.tensor.matmul(psum[0:2, u, :], act[:, k, :], wbuf[u][:, k, :],
                                                        start=k == 0, stop=k == KC - 1)
                            last.then_inc(mm_done, 1)

            @block.vector
            def _(dve):
                dve.sem_inc(row_done, NBUF)
                dve.wait_ge(bias_in, 16)
                steps = Counter(plus1)
                for layer in range(DEPTH):
                    for kind in (SC1, SC2):
                        v = bias[:, layer * MOD + kind * D:layer * MOD + (kind + 1) * D]
                        steps.link(dve, nc.vector.tensor_scalar(v, v, 1.0, None, ALU.add))
                for layer in range(DEPTH):
                    with dve.Fori(0, CH // NBUF) as i:
                        for u in range(NBUF):
                            dve.wait_ge(mm_done, i * NBUF + (NBUF + layer * CH + u + 1))
                            at = i * (NBUF * HALF) + (layer * MOD + u * HALF)
                            nc.vector.tensor_tensor(row[:, ds(at, HALF)], psum[0:2, u, :], bias[:, ds(at, HALF)],
                                                    ALU.add).then_inc(row_done, 1)


def modulated_transpose(nc, s, x, ident, ps, layer, a, mod, spare=0):
    hT = s.sb("hT", [P, KC, TOK])
    mods = s.sb("mods", [P, 4 * D + spare])
    sc, sh = (mods[:, n * 2 * D:(n + 1) * 2 * D].rearrange("p (c d) -> p c d", c=2) for n in range(2))
    h = [s.sb(f"h{u}", [P, D]) for u in range(2)]
    x_in, mod_in, h_step, h_ready, hT_ps, hT_done = (
        s.sem(n) for n in ("x_in", "mod_in", "h_step", "h_ready", "hT_ps", "hT_done"))
    load_x = layer == 0

    def sync(sp):
        for cond in (LAT, CON):
            sp.dma_start(sc[:, cond, :], mod_row(mod, layer, cond, SC1)).then_inc(mod_in, 16)
            sp.dma_start(sh[:, cond, :], mod_row(mod, layer, cond, SH1)).then_inc(mod_in, 16)
        if load_x:
            sp.dma_start(x[:, 0:CTX_TILES, :], a["ctx"].rearrange("(t p) d -> p t d", p=P)).then_inc(x_in, 16)
            sp.dma_start(x[:, CTX_TILES:, :], a["x"].rearrange("(t p) d -> p t d", p=P)).then_inc(x_in, 16)

    def vector(dve):
        dve.wait_ge(mod_in, 64)
        if load_x:
            dve.wait_ge(x_in, 32)
        steps = Counter(h_step)
        for first, pairs, cond in ((0, 1, CON), (1, 2, LAT)):
            with dve.Fori(0, pairs) as i:
                steps.loop(i, 2)
                for u in range(2):
                    if first:
                        dve.wait_ge(hT_ps, i * 2 + (2 * first + u - 1))
                    xt = x[:, ds(i * 2 + (2 * first + u), 1), :].rearrange("p a d -> p (a d)")
                    steps.link(dve, nc.vector.tensor_tensor(h[u][:], xt, sc[:, cond, :], ALU.mult))
                    nc.vector.tensor_tensor(h[u][:], h[u][:], sh[:, cond, :], ALU.add).then_inc(h_ready, 1)
                steps.end(pairs)

    def tensor(pe):
        with pe.Fori(0, TILES // 2) as i:
            for u in range(2):
                pe.wait_ge(h_ready, i * 2 + (u + 1))
                pe.wait_ge(hT_done, i * 2 + (u + 1))
                for k in range(KC):
                    last = nc.tensor.transpose(ps[:, 2 * u + k // 4, (k % 4) * P:(k % 4 + 1) * P],
                                               h[u][:, k * P:(k + 1) * P], ident)
                last.then_inc(hT_ps, 1)

    def scalar(act):
        act.sem_inc(hT_done, 2)
        with act.Fori(0, TILES // 2) as i:
            for u in range(2):
                act.wait_ge(hT_ps, i * 2 + (u + 1))
                nc.scalar.copy(hT[:, :, ds(i * (2 * P) + u * P, P)],
                               ps[:, 2 * u:2 * u + 2, :].rearrange("p b (k c) -> p (b k) c", c=P)).then_inc(hT_done, 1)

    return hT, mods, h, (h_ready, TILES), (hT_done, TILES + 2), sync, vector, tensor, scalar


def lru_mixer(nc, a, mod, projected, mixed, x, ident, wo):
    w_in = a["w_in"]
    NC = D_RNN // P
    whole = [[b for b in range(NB) if c * P < (b + 1) * LB <= (c + 1) * P] for c in range(NC)]
    with Stage(nc, "lru") as s:
        ps = s.ps("ps", [P, 8, HALF])
        WG = NB * 4 * LB
        hT, mods, h, (h_ready, h_all), (hT_done, hT_all), front_sync, front_vector, front_tensor, front_scalar = modulated_transpose(
            nc, s, x, ident, ps, 0, a, mod, WG - 4 * D)
        wg = mods[0:LBP, 0:WG].rearrange("p (b d n) -> p b d n", b=NB, d=2)
        x_chunk, g_chunk = (h[n][:, 0:TOK] for n in range(2))
        wx = [s.sb(f"wx{u}", [P, KC, 2 * P]) for u in range(2)]
        cols = s.sb("cols", [LB, NB, COLS])
        gbias = s.sb("gbias", [LB, NB, 4])
        decay = s.sb("decay", [LB, NB, 2, 3])
        lam = [s.sb(f"lam{n}", [LB, NB, 2]) for n in range(6)]
        LEN = PAD_L + CTX + PAD_R + PAD_L + SEQ + PAD_R
        LAT0 = CTX + PAD_R + PAD_L
        OUTS = LEN - (TAPS - 1)
        xpad = [s.sb(f"xpad{u}", [LB, LEN]) for u in range(2)]
        conv = s.sb("conv", [LB, OUTS])
        xc = [s.sb(f"xc{u}", [LBP, TOK]) for u in range(2)]
        gate = [s.sb(f"gate{u}", [LB, TOK]) for u in range(2)]
        tr, a2, th = ([s.sb(f"{n}{d}", [LB, TOK]) for d in range(2)] for n in ("tr", "a2", "th"))
        ti, av = ([[s.sb(f"{n}{u}{d}", [LB, TOK]) for d in range(2)] for u in range(2)] for n in ("ti", "av"))
        backward = s.sb("backward", [LB, TOK])
        y = [s.sb(f"y{u}", [LB, TOK]) for u in range(2)]
        px, pg, pr, pi = (ps[:, 2 * n:2 * n + 2, :].rearrange("p b n -> p (b n)") for n in range(4))
        cols_in, wg_in, e_done, prep_step, prep_done = (s.sem(n) for n in ("cols_in", "wg_in", "e_done", "prep_step", "prep_done"))
        w_ld, y_out = ([s.sem(f"{n}{u}") for u in range(2)] for n in ("w_ld", "y_out"))
        x_ps, g_ps, gate_done, v_done, root_done, step = (
            s.sem(n) for n in ("x_ps", "g_ps", "gate_done", "v_done", "root_done", "step"))
        x_copied, g_copied, conv_done, gates_ps, tanh_done, dec_done, roots_used, y_done = (
            s.sem(n) for n in ("x_copied", "g_copied", "conv_done", "gates_ps", "tanh_done", "dec_done", "roots_used", "y_done"))
        x_stored, g_stored = s.pool_dma_sem("x_stored"), s.pool_dma_sem("g_stored")
        ctx_ld, lat_ld, gate_ld = ([s.pool_dma_sem(f"{n}{u}") for u in range(2)] for n in ("ctx_ld", "lat_ld", "gate_ld"))
        halves = ((0, HALF), (HALF, TOK - HALF))

        def col(t, b, *at):
            v = t[:, ds(b, 1), at[0]:at[0] + 1] if len(at) == 1 else t[:, ds(b, 1), at[0], at[1]:at[1] + 1]
            return v.rearrange("p a c -> p (a c)")

        with nc.Block() as block:

            @block.sync
            def _(sp):
                front_sync(sp)
                for u in range(2):
                    sp.dma_start(wx[u][:], w_in[u]).then_inc(w_ld[u], 16)
                sp.dma_start(cols[:], a["lru_cols"]).then_inc(cols_in, 16)
                sp.wait_ge(h_ready, h_all)
                sp.dma_start(wg, a["gate_w"]).then_inc(wg_in, 16)
                with sp.Fori(0, NC // 2 - 1) as i:
                    for u in range(2):
                        sp.wait_ge(g_ps, i * 2 + (u + 1))
                        sp.dma_start(wx[u][:], w_in[ds(i * 2 + (u + 2), 1)].rearrange("b p k n -> (b p) k n")).then_inc(w_ld[u], 16)
                wo.load(sp)

            @block.gpsimd
            def _(pool):
                def to_dram(n, c, chunk, copied, stored):
                    pool.wait_ge(copied, c + 2)
                    pool.dma_start(projected[n, c * P:(c + 1) * P, :], chunk).then_inc(stored, 16)
                    pool.wait_ge(stored, (c + 1) * 16)

                for c in range(NC):
                    to_dram(1, c, x_chunk, x_copied, x_stored)
                    for b in whole[c]:
                        pool.wait_ge(conv_done, b + 1)
                        u, rows = b % 2, slice(b * LB, (b + 1) * LB)
                        pool.dma_start(xpad[u][:, PAD_L:PAD_L + CTX], projected[1, rows, 0:CTX]).then_inc(ctx_ld[u], 16)
                        pool.dma_start(xpad[u][:, PAD_L + LAT0:PAD_L + LAT0 + SEQ], projected[1, rows, CTX:TOK]).then_inc(lat_ld[u], 16)
                    to_dram(0, c, g_chunk, g_copied, g_stored)
                    for b in whole[c]:
                        pool.wait_ge(y_done, b + 1)
                        u, rows = b % 2, slice(b * LB, (b + 1) * LB)
                        pool.dma_start(gate[u][:], projected[0, rows, :]).then_inc(gate_ld[u], 16)

            @block.tensor
            def _(pe):
                def project(c, part, at, n):
                    dst, copied, done = (px, x_copied, x_ps) if part else (pg, g_copied, g_ps)
                    if at == 0:
                        pe.wait_ge(copied, c + 1)
                    for k in range(KC):
                        last = nc.tensor.matmul(dst[:, at:at + n], wx[c % 2][:, k, part * P:(part + 1) * P],
                                                hT[:, k, at:at + n], start=k == 0, stop=k == KC - 1)
                    if at:
                        last.then_inc(done, 1)

                def gates(b, d):
                    if d == 0:
                        pe.wait_ge(conv_done, b + 3)
                    pe.wait_ge(tanh_done, b * 2 + (d + 1))
                    for part, dst in ((0, pr), (1, pi)):
                        for at, n in halves:
                            last = nc.tensor.matmul(dst[0:LB, at:at + n], wg[:, b, d, part * LB:(part + 1) * LB],
                                                    xc[b % 2][:, at:at + n], start=True, stop=True)
                    last.then_inc(gates_ps, 1)

                pe.sem_inc(gates_ps, 4)
                front_tensor(pe)
                pe.wait_ge(hT_done, hT_all)
                ready = []
                for c in range(NC):
                    pe.wait_ge(w_ld[c % 2], (c // 2 + 1) * 16)
                    if c == 1:
                        pe.wait_ge(wg_in, 16)
                    for n, (part, (at, size)) in enumerate((part, half) for part in (1, 0) for half in halves):
                        project(c, part, at, size)
                        if ready and (n % 2 == 0 or len(ready) > (3 - n) // 2):
                            gates(*ready.pop(0))
                    assert not ready
                    ready = [(b, d) for b in whole[c] for d in range(2)]
                for b, d in ready:
                    gates(b, d)

            @block.scalar
            def _(act):
                def copy_chunk(c, done, src, chunk, copied, stored):
                    act.wait_ge(done, c + 1)
                    if c:
                        act.wait_ge(stored, c * 16)
                    nc.scalar.copy(chunk, src[:, 0:TOK]).then_inc(copied, 1)

                def store(b):
                    act.dma_start(mixed[b * LB:(b + 1) * LB, :], y[b % 2][:]).then_inc(y_out[b % 2], 16)

                def direction(b, d):
                    u = b % 2
                    if d == 0:
                        act.wait_ge(y_done, b + 1)
                        if b >= 2:
                            store(b - 2)
                    act.wait_ge(gates_ps, b * 2 + (4 + d + 1))
                    act.wait_ge(dec_done, b * 2 + (d + 1))
                    nc.scalar.activation(tr[d][:], pr[0:LB, 0:TOK], ACT.Tanh, scale=0.5, bias=gbias[:, b, 2 * d:2 * d + 1])
                    nc.scalar.activation(ti[u][d][:], pi[0:LB, 0:TOK], ACT.Tanh, scale=0.5,
                                         bias=gbias[:, b, 2 * d + 1:2 * d + 2]).then_inc(tanh_done, 1)
                    act.wait_ge(tanh_done, b * 2 + (d + 2))
                    act.wait_ge(roots_used, b + 1)
                    n, minus, twice = (decay[:, b, d, j:j + 1] for j in range(3))
                    nc.scalar.activation(av[u][d][:], tr[d][:], ACT.Exp, scale=n, bias=n)
                    nc.scalar.activation(a2[d][:], tr[d][:], ACT.Exp, scale=twice, bias=twice)
                    nc.scalar.activation(th[d][:], tr[d][:], ACT.Tanh, scale=minus, bias=minus).then_inc(dec_done, 1)

                def roots_and_gate(b):
                    for d in range(2):
                        act.wait_ge(v_done, b * 2 + (d + 1))
                        nc.scalar.activation(th[d][:], th[d][:], ACT.Sqrt, scale=0.25).then_inc(root_done, 1)
                    act.wait_ge(gate_ld[b % 2], b // 2 * 16 + 16)
                    nc.scalar.activation(gate[b % 2][:], gate[b % 2][:], ACT.Gelu).then_inc(gate_done, 1)

                act.sem_inc(x_copied, 1)
                act.sem_inc(g_copied, 1)
                act.sem_inc(tanh_done, 1)
                act.sem_inc(dec_done, 2)
                front_scalar(act)
                act.wait_ge(cols_in, 16)
                nc.scalar.activation(lam[0][:], cols[:, :, 9:11], ACT.Abs).then_inc(e_done, 1)
                act.wait_ge(e_done, 1)
                nc.scalar.activation(lam[1][:], lam[0][:], ACT.Exp, scale=-1.0).then_inc(e_done, 1)
                for c in range(NC + 1):
                    blocks = whole[c - 1] if c else []
                    if c == 1:
                        act.wait_ge(prep_done, 1)
                    if blocks:
                        direction(blocks[0], 0)
                    if c < NC:
                        copy_chunk(c, x_ps, px, x_chunk, x_copied, x_stored)
                    if blocks:
                        direction(blocks[0], 1)
                        roots_and_gate(blocks[0])
                    if blocks[1:]:
                        direction(blocks[1], 0)
                    if c < NC:
                        copy_chunk(c, g_ps, pg, g_chunk, g_copied, g_stored)
                    if blocks[1:]:
                        direction(blocks[1], 1)
                        roots_and_gate(blocks[1])
                for b in (NB - 2, NB - 1):
                    act.wait_ge(y_done, b + 3)
                    store(b)
                for u in range(2):
                    act.wait_ge(y_out[u], NB // 2 * 16)

            @block.vector
            def _(dve):
                dve.sem_inc(y_done, 2)
                dve.sem_inc(roots_used, 1)
                for u in range(2):
                    nc.vector.memset(xc[u][:], 0.0)
                    nc.vector.memset(xpad[u][:], 0.0).then_inc(conv_done, 1)
                dve.wait_ge(conv_done, 2)
                front_vector(dve)
                dve.wait_ge(cols_in, 16)
                dve.wait_ge(e_done, 2)
                steps = Counter(prep_step)
                e, t, z, p, acc = lam[1], lam[2], lam[3], lam[4], lam[5]
                steps.link(dve, nc.vector.tensor_scalar(t[:], e[:], 2.0, None, ALU.add))
                steps.link(dve, nc.vector.reciprocal(t[:], t[:]))
                steps.link(dve, nc.vector.tensor_tensor(z[:], e[:], t[:], ALU.mult))
                steps.link(dve, nc.vector.tensor_tensor(p[:], z[:], z[:], ALU.mult))
                steps.link(dve, nc.vector.tensor_scalar(acc[:], p[:], 1.0 / 15, None, ALU.mult))
                for n in (13, 11, 9, 7, 5, 3):
                    steps.link(dve, nc.vector.scalar_tensor_tensor(acc[:], acc[:], 1.0 / n, p[:], ALU.add, ALU.mult))
                steps.link(dve, nc.vector.scalar_tensor_tensor(acc[:], acc[:], 1.0, z[:], ALU.add, ALU.mult))
                steps.link(dve, nc.vector.tensor_scalar(t[:], cols[:, :, 9:11], -1.0, 0.0, ALU.mult, ALU.max))
                steps.link(dve, nc.vector.scalar_tensor_tensor(acc[:], acc[:], 2.0, t[:], ALU.mult, ALU.add))
                for j, f in enumerate((-LRU_C / 2, LRU_C / 2, -LRU_C)):
                    nc.vector.tensor_scalar(decay[:, :, :, j], acc[:], f, None, ALU.mult)
                nc.vector.tensor_scalar(gbias[:], cols[:, :, 5:9], 0.5, None, ALU.mult).then_inc(prep_done, 1)
                dve.wait_ge(prep_done, 1)
                main = Counter(step)
                CONV_STEPS, SCAN_STEPS = 3, 8

                def convolve(i, u):
                    b = i * 2 + u
                    dve.wait_ge(ctx_ld[u], i * 16 + 16)
                    dve.wait_ge(lat_ld[u], i * 16 + 16)
                    main.link(dve, nc.vector.tensor_scalar(conv[:], xpad[u][:, 0:OUTS], col(cols, b, 0), col(cols, b, TAPS),
                                                           ALU.mult, ALU.add))
                    for k in (1, 2):
                        main.link(dve, nc.vector.scalar_tensor_tensor(conv[:], xpad[u][:, k:k + OUTS], col(cols, b, k),
                                                                      conv[:], ALU.mult, ALU.add))
                    dve.wait_ge(gates_ps, b * 2 + 2)
                    k = TAPS - 1
                    for to, at, n in ((0, 0, CTX), (CTX, LAT0, SEQ)):
                        last = nc.vector.scalar_tensor_tensor(xc[u][0:LB, to:to + n], xpad[u][:, at + k:at + k + n],
                                                              col(cols, b, k), conv[:, at:at + n], ALU.mult, ALU.add)
                    last.then_inc(conv_done, 1)
                    dve.wait_ge(conv_done, b + 3)

                def scan(i, u, stores):
                    b = i * 2 + u
                    for d in range(2):
                        dve.wait_ge(dec_done, b * 2 + (d + 3))
                        nc.vector.scalar_tensor_tensor(th[d][:], a2[d][:], 1.0, th[d][:], ALU.add, ALU.mult).then_inc(v_done, 1)
                    for d in range(2):
                        main.link(dve, nc.vector.scalar_tensor_tensor(ti[u][d][:], ti[u][d][:], 1.0, xc[u][0:LB, :], ALU.add, ALU.mult))
                    for d in range(2):
                        dve.wait_ge(root_done, b * 2 + (d + 1))
                        main.link(dve, nc.vector.tensor_tensor(ti[u][d][:], ti[u][d][:], th[d][:], ALU.mult))
                    dve.sem_inc(roots_used, 1)
                    if stores is not None:
                        dve.wait_ge(y_out[u], stores * 16)
                    a0, a1, b0, b1 = av[u][0], av[u][1], ti[u][0], ti[u][1]
                    main.link(dve, nc.vector.tensor_tensor_scan(y[u][:], a0[:], b0[:], 0.0, ALU.mult, ALU.add))
                    main.link(dve, nc.vector.tensor_tensor_scan(backward[:, CTX - 1::-1], a1[:, CTX - 1::-1],
                                                                b1[:, CTX - 1::-1], 0.0, ALU.mult, ALU.add))
                    main.link(dve, nc.vector.tensor_tensor_scan(backward[:, TOK - 1:CTX - 1:-1], a1[:, TOK - 1:CTX - 1:-1],
                                                                b1[:, TOK - 1:CTX - 1:-1], backward[:, 0:1], ALU.mult, ALU.add))
                    main.link(dve, nc.vector.tensor_tensor(y[u][:], y[u][:], backward[:], ALU.add))
                    dve.wait_ge(gate_done, b + 1)
                    nc.vector.tensor_tensor(y[u][:], y[u][:], gate[u][:], ALU.mult).then_inc(y_done, 1)

                convolve(0, 0)
                convolve(0, 1)
                scan(0, 0, None)
                convolve(1, 0)
                scan(0, 1, None)
                with dve.Fori(0, NB // 2 - 2) as i:
                    main.loop(i, 2 * (CONV_STEPS + SCAN_STEPS))
                    convolve(i + 1, 1)
                    scan(i + 1, 0, i + 1)
                    convolve(i + 2, 0)
                    scan(i + 1, 1, i + 1)
                main.end(NB // 2 - 2)
                end = NB // 2 - 1
                convolve(end, 1)
                scan(end, 0, end)
                scan(end, 1, end)


def attn_mixer(nc, a, mod, mixed, x, ident, wo):
    PER_KV = HEADS // KV
    QT = SEQ // P
    with Stage(nc, "attn") as s:
        ps = s.ps("ps", [P, 8, HALF])
        hT, mods, _, _, (hT_done, hT_all), front_sync, front_vector, front_tensor, front_scalar = modulated_transpose(
            nc, s, x, ident, ps, 1, a, mod)
        wk, wv = s.sb("wk", [P, KC, KV * HD]), s.sb("wv", [P, KC, KV * HD])
        wq = [s.sb(f"wq{u}", [P, KC, HD]) for u in range(2)]
        rope, rot, ones, gains, eps = (s.sb("rope", [P, 2, TOK]), s.sb("rot", [P, P]), s.sb("ones", [P, P]),
                                       s.sb("gains", [P, 2]), s.sb("eps", [P, 1]))
        kT = [s.sb(f"kT{n}", [P, TOK]) for n in range(KV)]
        v = s.sb("v", [P, TILES, KV * HD])
        q_rows = s.sb("q_rows", [P, HEADS, SEQ])
        qT = [s.sb(f"qT{u}", [P, SEQ]) for u in range(2)]
        scaled, square, root, turned = ([mods[:, (2 * n + u) * HALF:(2 * n + u + 1) * HALF] for u in range(2)] for n in range(4))
        p = [s.sb(f"p{q}", [P, TOK]) for q in range(QT)]
        pT = s.sb("pT", [P, TILES, SEQ])
        biggest, neg_max, total, inv = (s.sb(n, [P, QT]) for n in ("biggest", "neg_max", "total", "inv"))
        o = [s.sb(f"o{u}", [P, SEQ]) for u in range(2)]
        const_in, ones_done, k_in, v_in, o_out = (s.sem(n) for n in ("const_in", "ones_done", "k_in", "v_in", "o_out"))
        wq_in = [s.sem(f"wq_in{u}") for u in range(2)]
        v_ps, v_copied, proj_ps, scaled_done, sums_ps, root_done, rows_done, q_ready = (
            s.sem(n) for n in ("v_ps", "v_copied", "proj_ps", "scaled_done", "sums_ps", "root_done", "rows_done", "q_ready"))
        step, max_done, norm_done = (s.sem(n) for n in ("step", "max_done", "norm_done"))
        s_ps, p_done, pT_ps, pT_copied, o_ps, o_copied, o_stored = (
            s.sem(n) for n in ("s_ps", "p_done", "pT_ps", "pT_copied", "o_ps", "o_copied", "o_stored"))
        proj, sums, partner = ([ps[:, 2 * n + u, :] for u in range(2)] for n in (1, 2, 3))
        out_ps = ps[:, 6, :]
        key_parts = ((0, HALF), (HALF, TOK - HALF))
        key_rows = [(n_kv, tokens, n) for n_kv in range(KV) for tokens, n in key_parts]
        K = len(key_rows)
        SCALE = HD ** -0.5

        def head_at(i, u):
            return i + u * PER_KV

        with nc.Block() as block:

            @block.sync
            def _(sp):
                front_sync(sp)
                sp.dma_start(wv[:], a["attn_wv"]).then_inc(v_in, 16)
                sp.dma_start(gains[:], a["gains"]).then_inc(const_in, 16)
                sp.dma_start(rot[:], a["rot"]).then_inc(const_in, 16)
                sp.dma_start(rope[:], a["rope"]).then_inc(const_in, 16)
                sp.dma_start(wk[:], a["attn_wk"]).then_inc(k_in, 16)
                with sp.Fori(0, HEADS // 2) as i:
                    for u in range(2):
                        sp.wait_ge(proj_ps, i * 2 + (u + K - 1))
                        sp.dma_start(wq[u][:], a["attn_wq"][ds(head_at(i, u), 1)].rearrange("h p k n -> (h p) k n")).then_inc(wq_in[u], 16)
                wo.load(sp)
                sp.sem_inc(o_stored, 2)
                with sp.Fori(0, HEADS // 2) as i:
                    for u in range(2):
                        sp.wait_ge(o_copied, i * 2 + (u + 2))
                        sp.dma_start(mixed[ds(i * HD + u * (PER_KV * HD), HD), 0:SEQ], o[u][:]).then_inc(o_out, 16)
                        sp.wait_ge(o_out, i * 32 + (16 * u + 16))
                        sp.sem_inc(o_stored, 1)

            @block.gpsimd
            def _(pool):
                with pool.Fori(0, HEADS // 2) as i:
                    for u in range(2):
                        pool.wait_ge(rows_done, i * 2 + (u + K + 1))
                        pool.wait_ge(s_ps, i * (2 * QT) + (u + 1) * QT)
                        nc.gpsimd.tensor_copy(qT[u][:], q_rows[:, ds(i * 2 + u, 1), :].rearrange("p h n -> p (h n)")).then_inc(q_ready, 1)

            @block.tensor
            def _(pe):
                def project(w, n, tokens, u):
                    for k in range(KC):
                        last = nc.tensor.matmul(proj[u][:, 0:n], w(k), hT[:, k, tokens:tokens + n], start=k == 0, stop=k == KC - 1)
                    last.then_inc(proj_ps, 1)

                def sums_and_partner(n, u, row):
                    pe.wait_ge(scaled_done, row + 1)
                    nc.tensor.matmul(sums[u][:, 0:n], ones[:], square[u][:, 0:n], start=True, stop=True)
                    nc.tensor.matmul(partner[u][:, 0:n], rot[:], scaled[u][:, 0:n], start=True, stop=True).then_inc(sums_ps, 1)

                def project_head(i, u):
                    pe.wait_ge(wq_in[u], i * 16 + 16)
                    pe.wait_ge(scaled_done, i * 2 + (K + u - 1))
                    project(lambda k: wq[u][:, k, :], SEQ, CTX, u)

                def finish_head(i, u):
                    pe.wait_ge(rows_done, i * 2 + (K + u - 1))
                    sums_and_partner(SEQ, u, i * 2 + (K + u))

                def score(i, u, q):
                    if q == 0:
                        pe.wait_ge(q_ready, i * 2 + (u + 1))
                    pe.wait_ge(p_done, i * (2 * QT) + (u * QT + q + 1))
                    for tokens, n in key_parts:
                        last = nc.tensor.matmul(ps[:, 2 * (q % 2) + tokens // HALF, 0:n], qT[u][:, q * P:(q + 1) * P],
                                                kT[u][:, tokens:tokens + n], start=True, stop=True)
                    last.then_inc(s_ps, 1)

                def turn(i, u, q):
                    pe.wait_ge(norm_done, i * (2 * QT) + (u * QT + q + 1))
                    pe.wait_ge(pT_copied, i * (2 * QT) + (u * QT + q + 1))
                    for t in range(TILES):
                        last = nc.tensor.transpose(ps[:, 4 + t // 4, (t % 4) * P:(t % 4 + 1) * P], p[q][:, t * P:(t + 1) * P], ident)
                    last.then_inc(pT_ps, 1)

                def values(i, u):
                    pe.wait_ge(pT_copied, i * (2 * QT) + ((u + 1) * QT + 1))
                    pe.wait_ge(o_copied, i * 2 + (u + 1))
                    for t in range(TILES):
                        last = nc.tensor.matmul(out_ps, v[:, t, u * HD:(u + 1) * HD], pT[:, t, :], start=t == 0, stop=t == TILES - 1)
                    last.then_inc(o_ps, 1)

                def head(i, u, following):
                    for q in range(2):
                        score(i, u, q + 2)
                        turn(i, u, q)
                    if following:
                        score(*following, 0)
                    turn(i, u, 2)
                    turn(i, u, 3)
                    if following:
                        score(*following, 1)
                    values(i, u)

                pe.sem_inc(s_ps, 2 * QT)
                pe.sem_inc(pT_ps, QT)
                pe.sem_inc(o_ps, 1)
                front_tensor(pe)
                pe.wait_ge(hT_done, hT_all)
                pe.wait_ge(v_in, 16)
                for t in range(TILES):
                    if t >= 2:
                        pe.wait_ge(v_copied, t - 1)
                    for k in range(KC):
                        last = nc.tensor.matmul(ps[:, t % 2, 0:KV * HD], hT[:, k, t * P:(t + 1) * P], wv[:, k, :],
                                                start=k == 0, stop=k == KC - 1)
                    last.then_inc(v_ps, 1)
                pe.wait_ge(k_in, 16)
                pe.wait_ge(const_in, 48)
                pe.wait_ge(ones_done, 2)
                for row, (n_kv, tokens, n) in enumerate(key_rows):
                    if row >= 2:
                        pe.wait_ge(scaled_done, row - 1)
                    project(lambda k: wk[:, k, n_kv * HD:(n_kv + 1) * HD], n, tokens, row % 2)
                    if row >= 1:
                        if row >= 3:
                            pe.wait_ge(rows_done, row - 2)
                        sums_and_partner(key_rows[row - 1][2], (row - 1) % 2, row - 1)
                project_head(0, 0)
                pe.wait_ge(rows_done, K - 2)
                sums_and_partner(key_rows[K - 1][2], (K - 1) % 2, K - 1)
                with pe.Fori(0, HEADS // 2 - 1) as i:
                    project_head(i, 1)
                    finish_head(i, 0)
                    project_head(i + 1, 0)
                    finish_head(i, 1)
                end = HEADS // 2 - 1
                project_head(end, 1)
                finish_head(end, 0)
                finish_head(end, 1)
                pe.wait_ge(v_copied, TILES)
                pe.wait_ge(rows_done, K + HEADS)
                score(0, 0, 0)
                score(0, 0, 1)
                with pe.Fori(0, HEADS // 2 - 1) as i:
                    head(i, 0, (i, 1))
                    head(i, 1, (i + 1, 0))
                head(end, 0, (end, 1))
                head(end, 1, None)

            @block.scalar
            def _(act):
                def rows(which, n, u, row):
                    act.wait_ge(proj_ps, row + 1)
                    nc.scalar.mul(scaled[u][:, 0:n], proj[u][:, 0:n], gains[:, which:which + 1])
                    nc.scalar.activation(square[u][:, 0:n], proj[u][:, 0:n], ACT.Square).then_inc(scaled_done, 1)
                    act.wait_ge(sums_ps, row + 1)
                    nc.scalar.activation(root[u][:, 0:n], sums[u][:, 0:n], ACT.Sqrt, bias=eps[:], scale=1.0 / HD).then_inc(root_done, 1)

                def exponentials(i, u, q):
                    act.wait_ge(max_done, i * (2 * QT) + (u * QT + q + 1))
                    act.wait_ge(pT_ps, i * (2 * QT) + (u * QT + q + 1))
                    b = 2 * (q % 2)
                    nc.scalar.activation(p[q][:], ps[:, b:b + 2, :].rearrange("p b n -> p (b n)")[:, 0:TOK], ACT.Exp,
                                         bias=neg_max[:, q:q + 1], scale=SCALE, accum_out=total[:, q:q + 1]).then_inc(p_done, 1)

                def copy_tile(i, u, q):
                    act.wait_ge(pT_ps, i * (2 * QT) + (u * QT + q + QT + 1))
                    act.wait_ge(o_ps, i * 2 + (u + 1))
                    nc.scalar.copy(pT[:, :, q * P:(q + 1) * P],
                                   ps[:, 4:6, :].rearrange("p b (t c) -> p (b t) c", c=P)[:, 0:TILES, :]).then_inc(pT_copied, 1)

                def head(i, u, following):
                    for q in range(2):
                        exponentials(i, u, q + 2)
                        copy_tile(i, u, q)
                    if following:
                        exponentials(*following, 0)
                    copy_tile(i, u, 2)
                    copy_tile(i, u, 3)
                    if following:
                        exponentials(*following, 1)
                    act.wait_ge(o_ps, i * 2 + (u + 2))
                    act.wait_ge(o_stored, i * 2 + (u + 1))
                    nc.scalar.copy(o[u][:], out_ps).then_inc(o_copied, 1)

                act.sem_inc(p_done, 2)
                act.sem_inc(pT_copied, 1)
                act.sem_inc(o_copied, 1)
                front_scalar(act)
                for t in range(TILES):
                    act.wait_ge(v_ps, t + 1)
                    nc.scalar.copy(v[:, t, :], ps[:, t % 2, 0:KV * HD]).then_inc(v_copied, 1)
                act.wait_ge(const_in, 48)
                act.wait_ge(ones_done, 2)
                for row, (_, _, n) in enumerate(key_rows):
                    if row >= 2:
                        act.wait_ge(rows_done, row - 1)
                    rows(1, n, row % 2, row)
                with act.Fori(0, HEADS // 2) as i:
                    for u in range(2):
                        act.wait_ge(rows_done, i * 2 + (K + u - 1))
                        rows(0, SEQ, u, i * 2 + (K + u))
                exponentials(0, 0, 0)
                exponentials(0, 0, 1)
                end = HEADS // 2 - 1
                with act.Fori(0, end) as i:
                    head(i, 0, (i, 1))
                    head(i, 1, (i + 1, 0))
                head(end, 0, (end, 1))
                head(end, 1, None)

            @block.vector
            def _(dve):
                nc.vector.memset(ones[:], 1.0).then_inc(ones_done, 1)
                nc.vector.memset(eps[:], EPS).then_inc(ones_done, 1)
                front_vector(dve)
                dve.wait_ge(const_in, 48)
                steps = Counter(step)

                def rows(out, n, tokens, u, row):
                    dve.wait_ge(sums_ps, row + 1)
                    steps.mark(nc.vector.tensor_tensor(turned[u][:, 0:n], partner[u][:, 0:n], rope[:, 1, tokens:tokens + n], ALU.mult))
                    steps.link(dve, nc.vector.tensor_tensor(out, scaled[u][:, 0:n], rope[:, 0, tokens:tokens + n], ALU.mult))
                    dve.wait_ge(root_done, row + 1)
                    steps.mark(nc.vector.reciprocal(root[u][:, 0:n], root[u][:, 0:n]))
                    steps.link(dve, nc.vector.tensor_tensor(out, out, turned[u][:, 0:n], ALU.add))
                    nc.vector.tensor_tensor(out, out, root[u][:, 0:n], ALU.mult).then_inc(rows_done, 1)

                def maximum(i, u, q):
                    b = 2 * (q % 2)
                    dve.wait_ge(s_ps, i * (2 * QT) + (u * QT + q + 2 * QT + 1))
                    steps.link(dve, nc.vector.tensor_reduce(biggest[:, q:q + 1], ps[:, b:b + 2, :].rearrange("p b n -> p (b n)")[:, 0:TOK],
                                                            AX_X, ALU.max))
                    nc.vector.tensor_scalar(neg_max[:, q:q + 1], biggest[:, q:q + 1], -SCALE, None, ALU.mult).then_inc(max_done, 1)

                def normalise(i, u, q):
                    dve.wait_ge(p_done, i * (2 * QT) + (u * QT + q + 3))
                    steps.link(dve, nc.vector.reciprocal(inv[:, q:q + 1], total[:, q:q + 1]))
                    nc.vector.tensor_scalar(p[q][:], p[q][:], inv[:, q:q + 1], None, ALU.mult).then_inc(norm_done, 1)

                def head(i, u, following):
                    for q in range(2):
                        normalise(i, u, q)
                        maximum(i, u, q + 2)
                    normalise(i, u, 2)
                    if following:
                        maximum(*following, 0)
                    normalise(i, u, 3)
                    if following:
                        maximum(*following, 1)

                for row, (n_kv, tokens, n) in enumerate(key_rows):
                    rows(kT[n_kv][:, tokens:tokens + n], n, tokens, row % 2, row)
                with dve.Fori(0, HEADS // 2) as i:
                    steps.loop(i, 2 * 4)
                    for u in range(2):
                        rows(q_rows[:, ds(i * 2 + u, 1), :].rearrange("p h n -> p (h n)"), SEQ, CTX, u, i * 2 + (K + u))
                steps.end(HEADS // 2)
                maximum(0, 0, 0)
                maximum(0, 0, 1)
                end = HEADS // 2 - 1
                with dve.Fori(0, end) as i:
                    steps.loop(i, 2 * QT * 2)
                    head(i, 0, (i, 1))
                    head(i, 1, (i + 1, 0))
                steps.end(end)
                head(end, 0, (end, 1))
                head(end, 1, None)


def token_stages(layer):
    if layer == 0:
        return TILES, 0, ((0, 1, CON), (1, 2, LAT))
    return TILES - CTX_TILES, CTX_TILES, ((0, 2, LAT),)


NORM_STEPS = 7


def post_norm(nc, dve, steps, x_tile, update, gain, r, stats, mv, ln, read_done, var_done, root_done):
    nc.vector.tensor_tensor(r, update, gain, ALU.mult).then_inc(read_done[0], 1)
    dve.wait_ge(*read_done)
    steps.link(dve, nc.vector.scalar_tensor_tensor(r, x_tile, ALPHA, r, ALU.mult, ALU.add))
    for n in range(2):
        steps.mark(nc.vector.bn_stats(stats[:, n, :], r[:, n * HALF:(n + 1) * HALF]))
    steps.wait(dve)
    nc.vector.memset(mv[:, 2:3], EPS)
    steps.link(dve, nc.vector.bn_aggr(mv[:, 0:2], stats[:].rearrange("p a b -> p (a b)")))
    nc.vector.tensor_tensor(mv[:, 2:3], mv[:, 1:2], mv[:, 2:3], ALU.add).then_inc(var_done, 1)
    dve.wait_ge(*root_done)
    steps.link(dve, nc.vector.reciprocal(mv[:, 4:5], mv[:, 3:4]))
    steps.link(dve, nc.vector.tensor_scalar(r, r, mv[:, 0:1], mv[:, 4:5], ALU.subtract, ALU.mult))
    steps.link(dve, nc.vector.tensor_tensor(r, r, ln[:, 0, :], ALU.mult))
    return nc.vector.tensor_tensor(x_tile, r, ln[:, 1, :], ALU.add)


def post_mixer(nc, a, mod, mixed, h2, scores, x, ident, layer, out_weights):
    T, x_first, streams = token_stages(layer)
    wo, CH = out_weights.w, out_weights.chunks
    src = mixed.rearrange("(k p) n -> p k n", p=P)
    dst = scores[0:T * PH].rearrange("(t h) p s k -> h s p t k", h=PH)
    halves = [(at, min(HALF, T * P - at)) for at in range(0, T * P, HALF)]
    with Stage(nc, f"post{layer}") as s:
        ps = s.ps("ps", [P, 8, HALF])
        mt = [s.sb(f"mt{u}", [P, CH, P]) for u in range(2)]
        rows = s.sb("rows", [P, 2, 3, D])
        ln = s.sb("ln", [P, 2, D])
        r = s.sb("r", [P, D])
        stats = s.sb("stats", [P, 2, 6])
        mv = s.sb("mv", [P, 5])
        h2b = [s.sb(f"h2b{u}", [P, D]) for u in range(2)]
        h2T = s.sb("h2T", [P, KC, T * P])
        wq = [s.sb(f"wq{u}", [P, KC, P]) for u in range(2)]
        keys = s.sb("keys", [P, 2, NK])
        qT = [s.sb(f"qT{u}", [P, T * P]) for u in range(2)]
        sb = [s.sb(f"sb{u}", [P, T, NK]) for u in range(2)]
        rows_in, keys_in = s.sem("rows_in"), s.sem("keys_in")
        h2_out, s_out, wrap_out = (s.pool_dma_sem(n) for n in ("h2_out", "s_out", "wrap_out"))
        mt_in, wq_in = ([s.sem(f"{n}{u}") for u in range(2)] for n in ("mt_in", "wq_in"))
        step, var_done, root_done, h2_ready, h2T_ps = (
            s.sem(n) for n in ("step", "var_done", "root_done", "h2_ready", "h2T_ps"))
        y_ps, y_read, h2_stored, h2T_done, q_ps, q_copied, s_ps, s_copied, s_stored = (
            s.sem(n) for n in ("y_ps", "y_read", "h2_stored", "h2T_done", "q_ps", "q_copied", "s_ps", "s_copied", "s_stored"))
        with nc.Block() as block:

            @block.sync
            def _(sp):
                for u in range(2):
                    sp.dma_start(mt[u][:], src[:, 0:CH, u * P:(u + 1) * P]).then_inc(mt_in[u], 16)
                for c in sorted({c for _, _, c in streams}):
                    for j, kind in enumerate((G1, SC2, SH2)):
                        sp.dma_start(rows[:, c, j, :], mod_row(mod, layer, c, kind)).then_inc(rows_in, 16)
                sp.dma_start(ln[:, 0, :], row_of(a["ln_g"][layer, 0])).then_inc(rows_in, 16)
                sp.dma_start(ln[:, 1, :], row_of(a["ln_b"][layer, 0])).then_inc(rows_in, 16)
                sp.dma_start(keys[:], a["sub_keys"][layer]).then_inc(keys_in, 16)
                for u in range(2):
                    sp.dma_start(wq[u][:], a["peer_wq"][layer, u]).then_inc(wq_in[u], 16)
                with sp.Fori(0, T // 2 - 1) as i:
                    for u in range(2):
                        sp.wait_ge(y_ps, i * 2 + (u + 3))
                        sp.dma_start(mt[u][:], src[:, 0:CH, ds(i * (2 * P) + (u + 2) * P, P)]).then_inc(mt_in[u], 16)
                with sp.Fori(0, PH - 1) as i:
                    for u in range(2):
                        sp.wait_ge(q_ps, i * 2 + (u + 3))
                        sp.dma_start(wq[u][:], a["peer_wq"][layer, ds(i * 2 + (u + 2), 1)].rearrange("h p k n -> (h p) k n")).then_inc(wq_in[u], 16)

            @block.gpsimd
            def _(pool):
                pool.sem_inc(h2_stored, 2)
                pool.sem_inc(s_stored, 2)
                with pool.Fori(0, T // 2) as i:
                    for u in range(2):
                        pool.wait_ge(h2_ready, i * 2 + (u + 1))
                        pool.dma_start(h2[ds(i * 2 + u, 1)].rearrange("t p d -> (t p) d"), h2b[u][:]).then_inc(h2_out, 16)
                        pool.wait_ge(h2_out, i * 32 + (16 * u + 16))
                        pool.sem_inc(h2_stored, 1)
                with pool.Fori(0, PH) as i:
                    for u in range(2):
                        pool.wait_ge(s_copied, i * 2 + (u + 3))
                        pool.dma_start(dst[ds(i, 1), u].rearrange("h p t k -> (h p) t k"), sb[u][:]).then_inc(s_out, 16)
                        pool.wait_ge(s_out, i * 32 + (16 * u + 16))
                        pool.sem_inc(s_stored, 1)
                pool.dma_start(scores[T * PH:T * PH + 2], scores[0:2]).then_inc(wrap_out, 16)
                pool.wait_ge(wrap_out, 16)

            @block.tensor
            def _(pe):
                pe.sem_inc(y_ps, 2)
                pe.sem_inc(q_ps, 2)
                pe.sem_inc(s_ps, 2)
                pe.wait_ge(out_weights.loaded, 16)

                def project(i, u):
                    pe.wait_ge(mt_in[u], i * 16 + 16)
                    pe.wait_ge(y_read, i * 2 + (u + 1))
                    for h in range(2):
                        for k in range(CH):
                            last = nc.tensor.matmul(ps[:, 2 * u + h, :], mt[u][:, k, :], wo[:, k, h * HALF:(h + 1) * HALF],
                                                    start=k == 0, stop=k == CH - 1)
                    last.then_inc(y_ps, 1)

                def turn(i, u):
                    pe.wait_ge(h2_ready, i * 2 + (u + 1))
                    pe.wait_ge(h2T_done, i * 2 + (u + 1))
                    for k in range(KC):
                        last = nc.tensor.transpose(ps[:, 4 + 2 * u + k // 4, (k % 4) * P:(k % 4 + 1) * P],
                                                   h2b[u][:, k * P:(k + 1) * P], ident)
                    last.then_inc(h2T_ps, 1)

                project(0, 0)
                with pe.Fori(0, T // 2 - 1) as i:
                    project(i, 1)
                    turn(i, 0)
                    project(i + 1, 0)
                    turn(i, 1)
                project(T // 2 - 1, 1)
                turn(T // 2 - 1, 0)
                turn(T // 2 - 1, 1)
                pe.wait_ge(h2T_done, T + 2)
                pe.wait_ge(y_read, T + 2)
                pe.wait_ge(keys_in, 16)
                with pe.Fori(0, PH) as i:
                    for u in range(2):
                        pe.wait_ge(wq_in[u], i * 16 + 16)
                        pe.wait_ge(q_copied, i * 2 + (u + 1))
                        for h, (at, n) in enumerate(halves):
                            for k in range(KC):
                                last = nc.tensor.matmul(ps[:, 2 * u + h, 0:n], wq[u][:, k, :], h2T[:, k, at:at + n],
                                                        start=k == 0, stop=k == KC - 1)
                        last.then_inc(q_ps, 1)
                    for u in range(2):
                        pe.wait_ge(q_copied, i * 2 + (u + 3))
                        pe.wait_ge(s_copied, i * 2 + (u + 1))
                        for t in range(T):
                            last = nc.tensor.matmul(ps[:, 4 + 2 * u + t // 4, (t % 4) * P:(t % 4 + 1) * P],
                                                    qT[u][:, t * P:(t + 1) * P], keys[:, u, :], start=True, stop=True)
                        last.then_inc(s_ps, 1)

            @block.scalar
            def _(act):
                act.sem_inc(h2T_done, 2)
                act.sem_inc(q_copied, 2)
                with act.Fori(0, T // 2) as i:
                    for u in range(2):
                        act.wait_ge(var_done, i * 2 + (u + 1))
                        nc.scalar.activation(mv[:, 3:4], mv[:, 2:3], ACT.Sqrt).then_inc(root_done, 1)
                        act.wait_ge(h2T_ps, i * 2 + (u + 1))
                        nc.scalar.copy(h2T[:, :, ds(i * (2 * P) + u * P, P)],
                                       ps[:, 4 + 2 * u:6 + 2 * u, :].rearrange("p b (k c) -> p (b k) c", c=P)).then_inc(h2T_done, 1)
                with act.Fori(0, PH) as i:
                    for u in range(2):
                        act.wait_ge(q_ps, i * 2 + (u + 3))
                        act.wait_ge(s_ps, i * 2 + (u + 1))
                        nc.scalar.copy(qT[u][:], ps[:, 2 * u:2 * u + 2, :].rearrange("p b n -> p (b n)")[:, 0:T * P]).then_inc(q_copied, 1)

            @block.vector
            def _(dve):
                dve.sem_inc(y_read, 2)
                dve.sem_inc(s_copied, 2)
                dve.wait_ge(rows_in, 16 * (3 * len(streams) + 2))
                steps = Counter(step)
                for first, pairs, cond in streams:
                    with dve.Fori(0, pairs) as i:
                        steps.loop(i, 2 * (NORM_STEPS + 2))
                        for u in range(2):
                            t = i * 2 + (2 * first + u)
                            dve.wait_ge(y_ps, t + 3)
                            xt = x[:, ds(t + x_first, 1), :].rearrange("p a d -> p (a d)")
                            steps.link(dve, post_norm(nc, dve, steps, xt, ps[:, 2 * u:2 * u + 2, :].rearrange("p b n -> p (b n)"),
                                                      rows[:, cond, 0, :], r[:], stats, mv, ln, (y_read, t + 3), var_done,
                                                      (root_done, t + 1)))
                            dve.wait_ge(h2_stored, t + 1)
                            dve.wait_ge(h2T_done, t + 1)
                            steps.link(dve, nc.vector.tensor_tensor(h2b[u][:], xt, rows[:, cond, 1, :], ALU.mult))
                            nc.vector.tensor_tensor(h2b[u][:], h2b[u][:], rows[:, cond, 2, :], ALU.add).then_inc(h2_ready, 1)
                    steps.end(pairs)
                with dve.Fori(0, PH) as i:
                    for u in range(2):
                        dve.wait_ge(s_ps, i * 2 + (u + 3))
                        dve.wait_ge(s_stored, i * 2 + (u + 1))
                        nc.vector.tensor_copy(sb[u][:].rearrange("p t k -> p (t k)"),
                                              ps[:, 4 + 2 * u:6 + 2 * u, :].rearrange("p b n -> p (b n)")[:, 0:T * P]).then_inc(s_copied, 1)


def top16(nc, dve, steps, values, rest, top, at, hold):
    hold()
    steps.link(dve, nc.vector.max(top[:, 0:8], values))
    hold()
    steps.mark(nc.vector.max_index(at[:, 0:8], top[:, 0:8], values))
    steps.link(dve, nc.vector.match_replace(rest, top[:, 0:8], values, LOWEST))
    hold()
    steps.link(dve, nc.vector.max(top[:, 8:16], rest))
    hold()
    steps.link(dve, nc.vector.max_index(at[:, 8:16], top[:, 8:16], rest))


ROUTE_STEPS = 26


def peer(nc, a, mod, h2, scores, x, layer, out):
    T, x_first, streams = token_stages(layer)
    N = T * PH
    NJ = TOPK // BATCH
    conds = sorted({c for _, _, c in streams})
    with Stage(nc, f"peer{layer}") as s:
        acc = s.ps("acc", [P, 2, HALF])
        ring = s.sb("ring", [P, TOPK, ROW])
        h2b = [s.sb(f"h2b{u}", [P, D]) for u in range(2)]
        product = [s.sb(f"product{n}", [P, D]) for n in range(2)]
        diag = s.sb("diag", [P, TOPK, P])
        eye = s.sb("eye", [P, P])
        zero = s.sb("zero", [1, HALF], mybir.dt.bfloat16)
        g2 = s.sb("g2", [P, 2, D])
        ln = s.sb("ln", [P, 2, D])
        iota = s.sb("iota", [P, TOPK])
        stats, mv = s.sb("stats", [P, 2, 6]), s.sb("mv", [P, 5])
        scb = [s.sb(f"scb{u}", [P, 2, NK]) for u in range(2)]
        rest = s.sb("rest", [P, NK])
        cand, cand_rest = (s.sb(n, [P, TOPK * TOPK]) for n in ("cand", "cand_rest"))
        hot = s.sb("hot", [P, TOPK, TOPK])
        top = [s.sb(f"top{n}", [P, TOPK]) for n in range(3)]
        at = [s.sb(f"at{n}", [P, TOPK], U32) for n in range(3)]
        place, key = s.sb("place", [P, TOPK], U32), [s.sb(f"key{n}", [P, TOPK]) for n in range(2)]
        idx = [s.sb(f"idx{u}", [P, TOPK], U32) for u in range(2)]
        neg_max, total, inv = (s.sb(n, [P, 2]) for n in ("neg_max", "total", "inv"))
        expo, share, dots, gelu, weight = ([s.sb(f"{n}{u}", [P, TOPK]) for u in range(2)]
                                           for n in ("expo", "share", "dots", "gelu", "weight"))
        const_in, zero_done, idx_done, max_done, exp_done, step, sc_used = (
            s.sem(n) for n in ("const_in", "zero_done", "idx_done", "max_done", "exp_done", "step", "sc_used"))
        gelu_done, weight_done, diag_done, tile_ps, var_done, root_done, x_out = (
            s.sem(n) for n in ("gelu_done", "weight_done", "diag_done", "tile_ps", "var_done", "root_done", "x_out"))
        held, slots_granted, iota_in = s.sem("held"), s.sem("slots_granted"), s.sem("iota_in")
        row_in = [s.pool_dma_sem(f"row_in{k}") for k in range(TOPK)]
        sc_in = [s.sem(f"sc_in{u}") for u in range(2)]
        h2_in = [s.sem(f"h2_in{u}") for u in range(2)]
        row_used, dot_done, acc_read, x_done = (s.sem(n) for n in ("row_used", "dot_done", "acc_read", "x_done"))

        def tiles(eng):
            for first, pairs, cond in streams:
                with eng.Fori(0, pairs) as i:
                    for tu in range(2):
                        yield cond, tu, i * 2 + (2 * first + tu), i + first

        with nc.Block() as block:

            @block.sync
            def _(sp):
                for u in range(2):
                    sp.dma_start(scb[u][:], scores[u]).then_inc(sc_in[u], 16)
                sp.dma_start(iota[:], a["iota"].rearrange("(a n) -> a n", a=1).broadcast_to([P, TOPK])).then_inc(iota_in, 16)
                sp.dma_start(eye[:], a["eye"]).then_inc(const_in, 16)
                for c in conds:
                    sp.dma_start(g2[:, c, :], mod_row(mod, layer, c, G2)).then_inc(const_in, 16)
                sp.dma_start(ln[:, 0, :], row_of(a["ln_g"][layer, 1])).then_inc(const_in, 16)
                sp.dma_start(ln[:, 1, :], row_of(a["ln_b"][layer, 1])).then_inc(const_in, 16)
                for cond, tu, t, _ in tiles(sp):
                    sp.wait_ge(x_done, t + 1)
                    sp.dma_start(h2b[tu][:], h2[ds(t, 1)].rearrange("t p d -> (t p) d")).then_inc(h2_in[tu], 16)
                    with sp.Fori(0, PH // 2) as i:
                        for u in range(2):
                            sp.wait_ge(sc_used, t * PH + i * 2 + (u + 1))
                            sp.dma_start(scb[u][:], scores[ds(t * PH + i * 2 + (u + 2), 1)].rearrange("g p s k -> (g p) s k")).then_inc(sc_in[u], 16)

            @block.gpsimd
            def _(pool):
                with pool.Fori(0, N // 2) as i:
                    for u in range(2):
                        pool.wait_ge(idx_done, i * 2 + (u + 1))
                        for k in range(TOPK):
                            if k % BATCH == 0:
                                pool.wait_ge(row_used, i * (2 * TOPK) + (u * TOPK + k + BATCH))
                                pool.sem_inc(slots_granted, 1)
                            pool.indirect_dma_start(
                                out=ring[:, k, :], out_offset=None, in_=a["uv"],
                                in_offset=bass.IndirectOffsetOnAxis(ap=idx[u][:, k:k + 1], axis=0)).then_inc(row_in[k], 16)

            @block.vector
            def _(dve):
                dve.sem_inc(dot_done, 2)
                dve.sem_inc(acc_read, 1)
                dve.sem_inc(x_done, 2)
                nc.vector.memset(zero[:], 0.0).then_inc(zero_done, 1)
                steps = Counter(step)
                n_const = 16 * (3 + len(conds))

                def hold():
                    dve.sem_inc(held, 1)

                def route_half(u, n):
                    top16(nc, dve, steps, scb[u][:, n, :], rest[:], top[n][:], at[n][:], hold)

                def route_pairs(u, g):
                    grid = [P, TOPK, TOPK]
                    nc.vector.tensor_tensor(cand[:].rearrange("p (a b) -> p a b", b=TOPK),
                                            top[0][:].unsqueeze(2).broadcast_to(grid),
                                            top[1][:].unsqueeze(1).broadcast_to(grid), ALU.add).then_inc(sc_used, 1)
                    dve.wait_ge(sc_used, g + 1)
                    top16(nc, dve, steps, cand[:], cand_rest[:], top[2][:], at[2][:], hold)
                    nc.vector.tensor_scalar(neg_max[:, u:u + 1], top[2][:, 0:1], -1.0, None, ALU.mult).then_inc(max_done, 1)

                def route_experts(u):
                    grid = [P, TOPK, TOPK]
                    for n, (op, by) in enumerate(((ALU.logical_shift_right, 4), (ALU.bitwise_and, TOPK - 1))):
                        steps.link(dve, nc.vector.tensor_scalar(place[:], at[2][:], by, None, op))
                        steps.link(dve, nc.vector.tensor_tensor(hot[:], place[:].unsqueeze(2).broadcast_to(grid),
                                                                iota[:].unsqueeze(1).broadcast_to(grid), ALU.is_equal))
                        steps.link(dve, nc.vector.tensor_tensor(hot[:], hot[:], at[n][:].unsqueeze(1).broadcast_to(grid), ALU.mult))
                        steps.link(dve, nc.vector.tensor_reduce(key[n][:], hot[:], AX_X, ALU.add))
                    steps.link(dve, nc.vector.tensor_scalar(key[0][:], key[0][:], float(NK), float(layer * EXPERTS), ALU.mult, ALU.add))
                    nc.vector.tensor_tensor(idx[u][:], key[0][:], key[1][:], ALU.add).then_inc(idx_done, 1)

                def route_share(u, g):
                    dve.wait_ge(exp_done, g + 1)
                    steps.link(dve, nc.vector.reciprocal(inv[:, u:u + 1], total[:, u:u + 1]))
                    steps.link(dve, nc.vector.tensor_scalar(share[u][:], expo[u][:], inv[:, u:u + 1], None, ALU.mult))

                def dot_batch(u, tu, g, j):
                    for k in range(j * BATCH, (j + 1) * BATCH):
                        dve.wait_ge(row_in[k], (g + 1) * 16)
                        dve.wait_ge(dot_done, g * TOPK + (k + 1))
                        nc.vector.scalar_tensor_tensor(product[k % 2][:], ring[:, k, 0:D], 1.0, h2b[tu][:], ALU.mult, ALU.mult,
                                                       accum_out=dots[u][:, k:k + 1]).then_inc(dot_done, 1)

                def weigh_batch(u, g, j):
                    dve.wait_ge(gelu_done, g * NJ + (j + 1))
                    part = slice(j * BATCH, (j + 1) * BATCH)
                    nc.vector.tensor_tensor(weight[u][:, part], gelu[u][:, part], share[u][:, part], ALU.mult).then_inc(weight_done, 1)

                dve.wait_ge(iota_in, 16)
                for u in range(2):
                    dve.wait_ge(sc_in[u], 16)
                    route_half(u, 0)
                    route_half(u, 1)
                    route_pairs(u, u)
                    route_experts(u)
                    route_share(u, u)
                dve.wait_ge(const_in, n_const)
                hold()
                for cond, tu, t, pair in tiles(dve):
                    dve.wait_ge(h2_in[tu], pair * 16 + 16)
                    hold()
                    with dve.Fori(0, PH // 2) as i:
                        for u in range(2):
                            g = t * PH + i * 2 + u
                            steps.base, steps.n = g * ROUTE_STEPS + 2 * ROUTE_STEPS + t * NORM_STEPS, 0
                            dot_batch(u, tu, g, 0)
                            dve.wait_ge(sc_in[u], t * (PH // 2 * 16) + i * 16 + 32)
                            route_half(u, 0)
                            dot_batch(u, tu, g, 1)
                            weigh_batch(u, g, 0)
                            route_half(u, 1)
                            dot_batch(u, tu, g, 2)
                            weigh_batch(u, g, 1)
                            route_pairs(u, g + 2)
                            dot_batch(u, tu, g, 3)
                            weigh_batch(u, g, 2)
                            route_experts(u)
                            weigh_batch(u, g, 3)
                            route_share(u, g + 2)
                            assert steps.n == ROUTE_STEPS
                        hold()
                    steps.base, steps.n = (t + 1) * (PH * ROUTE_STEPS) + 2 * ROUTE_STEPS + t * NORM_STEPS, 0
                    dve.wait_ge(tile_ps, t + 1)
                    xt = x[:, ds(t + x_first, 1), :].rearrange("p a d -> p (a d)")
                    post_norm(nc, dve, steps, xt, acc[:].rearrange("p b n -> p (b n)"), g2[:, cond, :], product[0][:], stats,
                              mv, ln, (acc_read, t + 2), var_done, (root_done, t + 1)).then_inc(x_done, 1)
                    dve.wait_ge(x_done, t + 3)
                    hold()

            @block.scalar
            def _(act):
                def exponentials(u, g):
                    act.wait_ge(max_done, g + 1)
                    nc.scalar.activation(expo[u][:], top[2][:], ACT.Exp, bias=neg_max[:, u:u + 1],
                                         accum_out=total[:, u:u + 1]).then_inc(exp_done, 1)

                def gelu_batch(u, g, j):
                    act.wait_ge(dot_done, g * TOPK + ((j + 1) * BATCH + 2))
                    part = slice(j * BATCH, (j + 1) * BATCH)
                    nc.scalar.activation(gelu[u][:, part], dots[u][:, part], ACT.Gelu).then_inc(gelu_done, 1)

                def diag_batch(u, g, j):
                    act.wait_ge(weight_done, g * NJ + (j + 1))
                    act.wait_ge(row_used, g * TOPK + (j + 1) * BATCH)
                    for k in range(j * BATCH, (j + 1) * BATCH):
                        last = nc.scalar.mul(diag[:, k, :], eye[:], weight[u][:, k:k + 1])
                    last.then_inc(diag_done, 1)

                for u in range(2):
                    exponentials(u, u)
                for cond, tu, t, _ in tiles(act):
                    with act.Fori(0, PH // 2) as i:
                        for u in range(2):
                            g = t * PH + i * 2 + u
                            gelu_batch(u, g, 0)
                            gelu_batch(u, g, 1)
                            diag_batch(u, g, 0)
                            gelu_batch(u, g, 2)
                            diag_batch(u, g, 1)
                            exponentials(u, g + 2)
                            gelu_batch(u, g, 3)
                            diag_batch(u, g, 2)
                            diag_batch(u, g, 3)
                    act.wait_ge(var_done, t + 1)
                    nc.scalar.activation(mv[:, 3:4], mv[:, 2:3], ACT.Sqrt).then_inc(root_done, 1)
                    if out is not None:
                        act.wait_ge(x_done, t + 3)
                        xt = x[:, ds(t + x_first, 1), :].rearrange("p a d -> p (a d)")
                        act.dma_start(out[ds(t * P, P), :], xt).then_inc(x_out, 16)
                if out is not None:
                    act.wait_ge(x_out, 16 * T)

            @block.tensor
            def _(pe):
                pe.sem_inc(row_used, TOPK)
                pe.wait_ge(zero_done, 1)
                for cond, tu, t, _ in tiles(pe):
                    pe.wait_ge(acc_read, t + 1)
                    for h in range(2):
                        nc.tensor.matmul(acc[:, h, :], zero[:, 0:P], zero[:], start=True, stop=False)
                    with pe.Fori(0, PH // 2) as i:
                        for u in range(2):
                            for j in range(NJ):
                                pe.wait_ge(diag_done, t * (PH * NJ) + i * (2 * NJ) + (u * NJ + j + 1))
                                for k in range(j * BATCH, (j + 1) * BATCH):
                                    for h in range(2):
                                        last = nc.tensor.matmul(acc[:, h, :], diag[:, k, :],
                                                                ring[:, k, D + h * HALF:D + (h + 1) * HALF],
                                                                start=False, stop=False)
                                    last.then_inc(row_used, 1)
                    for h in range(2):
                        last = nc.tensor.matmul(acc[:, h, :], zero[:, 0:P], zero[:], start=False, stop=True)
                    last.then_inc(tile_ps, 1)



_OUT = ("out_dram", (1, SEQ, D))


def layout(i):
    c = np.ascontiguousarray
    cond = np.stack([i["c"][0], i["c_ctx"]], -1).reshape(KC, P, 2).transpose(1, 0, 2)
    w_in = i["lru_w_in"][0].reshape(KC, P, 2, D_RNN // P, P).transpose(3, 1, 0, 2, 4).reshape(D_RNN // P, P, KC, 2 * P)
    gate_w = np.zeros((LBP, NB, 2, 2 * LB), np.float32)
    gate_w[:LB] = i["lru_gate_w"][0].transpose(2, 1, 0, 3)
    gb = i["lru_gate_b"][0].reshape(2, NB, 2, LB).transpose(3, 1, 0, 2).reshape(LB, NB, 4)
    lru_cols = np.concatenate([
        i["lru_conv_w"][0].reshape(TAPS, NB, LB).transpose(2, 1, 0),
        i["lru_conv_b"][0].reshape(1, NB, LB).transpose(2, 1, 0),
        gb,
        i["lru_lambda"][0].reshape(2, NB, LB).transpose(2, 1, 0)], -1)
    uv = np.concatenate([i["peer_u"], i["peer_v"]], -1).reshape(DEPTH * EXPERTS, ROW)
    wq = i["peer_w_q"].reshape(DEPTH, KC, P, 2 * PH, P).transpose(0, 3, 2, 1, 4)
    qkv = i["attn_w_qkv"][0]
    n_q = HEADS * HD
    attn_wq = qkv[:, :n_q].reshape(KC, P, HEADS, HD).transpose(2, 1, 0, 3)
    attn_wk = qkv[:, n_q:n_q + KV * HD].reshape(KC, P, KV * HD).transpose(1, 0, 2)
    attn_wv = qkv[:, n_q + KV * HD:].reshape(KC, P, KV * HD).transpose(1, 0, 2)
    gains = np.stack([i["attn_q_gain"][0], i["attn_k_gain"][0]], -1)
    return {k: c(v) for k, v in {
        "x": i["x"][0], "ctx": i["ctx"][0], "cond": cond, "mod_w": i["mod_w"], "mod_b": i["mod_b"],
        "ln_g": i["ln_g"], "ln_b": i["ln_b"], "w_in": w_in, "gate_w": gate_w, "lru_cols": lru_cols,
        "lru_w_out": i["lru_w_out"][0], "attn_wq": attn_wq, "attn_wk": attn_wk, "attn_wv": attn_wv,
        "gains": gains, "attn_w_out": i["attn_w_out"][0], "peer_wq": wq,
        "sub_keys": i["peer_sub_keys"].transpose(0, 3, 1, 2), "uv": uv,
        "rope": rope_tables(), "rot": rope_rotation(), "eye": np.eye(P, dtype=np.float32), "iota": np.arange(TOPK, dtype=np.float32)}.items()}


GRID_W = 64
ROPE_THETA = 10000.0


def rope_tables():
    axis = HD // 2
    token = np.arange(SEQ)
    place = np.stack([token // GRID_W, token % GRID_W]).astype(np.float32)
    freq = np.float32(ROPE_THETA) ** (-np.arange(0, axis, 2, dtype=np.float32) / np.float32(axis))
    angle = place[:, None, None, :] * freq[None, None, :, None]
    angle = np.broadcast_to(angle, (2, 2, axis // 2, SEQ)).reshape(HD, SEQ)
    out = np.zeros((HD, 2, TOK), np.float32)
    out[:, 0, :CTX] = 1.0
    out[:, 0, CTX:], out[:, 1, CTX:] = np.cos(angle), np.sin(angle)
    return out


def rope_rotation():
    half = HD // 4
    rot = np.zeros((HD, HD), np.float32)
    for axis in range(2):
        for n in range(half):
            one, two = axis * 2 * half + n, axis * 2 * half + half + n
            rot[two, one] = -1.0
            rot[one, two] = 1.0
    return rot


def program(nc, a, out, upto=99):
    mod = nc.dram_tensor("mod_scratch", (2, DEPTH * MOD), F32, kind="Internal").ap()
    mixed = nc.dram_tensor("mixed_scratch", (D_RNN, TOK), F32, kind="Internal").ap()
    projected = nc.dram_tensor("projected_scratch", (2, D_RNN, TOK), F32, kind="Internal").ap()
    h2 = nc.dram_tensor("h2_scratch", (TILES, P, D), F32, kind="Internal").ap()
    scores = nc.dram_tensor("score_scratch", (TILES * PH + 2, P, 2, NK), F32, kind="Internal").ap()
    with nc.sbuf_tensor("x_all", [P, TILES, D], F32) as x, nc.sbuf_tensor("eye_sb", [P, P], F32) as ident, \
            nc.semaphore("eye_in") as eye_in:
        with nc.Block() as block:

            @block.sync
            def _(sp):
                sp.dma_start(ident[:], a["eye"]).then_inc(eye_in, 16)
                sp.wait_ge(eye_in, 16)

        modulation(nc, a, mod)
        if upto >= 1:
            with OutWeights(nc, a, 0) as wo:
                lru_mixer(nc, a, mod, projected, mixed, x, ident[:], wo)
                if upto >= 2:
                    post_mixer(nc, a, mod, mixed, h2, scores, x, ident[:], 0, wo)
        if upto >= 3:
            peer(nc, a, mod, h2, scores, x, 0, None)
        if upto >= 4:
            with OutWeights(nc, a, 1) as wo:
                attn_mixer(nc, a, mod, mixed, x, ident[:], wo)
                if upto >= 5:
                    post_mixer(nc, a, mod, mixed, h2, scores, x, ident[:], 1, wo)
        if upto >= 6:
            peer(nc, a, mod, h2, scores, x, 1, out)


def kernel(**inputs):
    import concourse.bacc as _bacc
    from concourse.bass_utils import run_bass_kernel_spmd as _run

    nc = _bacc.Bacc("TRN2", target_bir_lowering=False, num_devices=1)
    arrays, a = {}, {}
    for name, v in layout({k: np.asarray(v) for k, v in inputs.items()}).items():
        arrays[f"in_{name}"] = v
        a[name] = nc.dram_tensor(f"in_{name}", v.shape, F32, kind="ExternalInput").ap()
    name, shape = _OUT
    out = nc.dram_tensor(name, shape, F32, kind="ExternalOutput").ap()
    program(nc, a, out[0])
    r = _run(nc, [arrays], core_ids=[0])
    return r.results[0][name]
```
